# Optimizing a Trainium2 kernel written in Bass

```python
import jax, jax.numpy as jnp
from jax import lax
import numpy as np

D_MODEL = 2048
BATCH = 1
SEQ = 256
DEPTH = 1

CHUNK = 64
WINDOW = 128
WINDOW_CHUNKS = WINDOW // CHUNK

ATTN_WIDTH = D_MODEL // 2
ATTN_HEAD_DIM = 64
ATTN_HEADS = ATTN_WIDTH // ATTN_HEAD_DIM
ATTN_KV_HEADS = max(1, ATTN_HEADS // 8)
ATTN_KV_WIDTH = ATTN_KV_HEADS * ATTN_HEAD_DIM

RET_WIDTH = D_MODEL - ATTN_WIDTH
RET_HEADS = 4
RET_HEAD_DIM = RET_WIDTH // RET_HEADS

D_MIX = ATTN_WIDTH + RET_WIDTH
D_FF = ((8 * D_MODEL // 3 + 255) // 256) * 256
ROPE_BASE = 10000.0
EPS = 1e-6

IN_SPLITS = (ATTN_WIDTH, ATTN_KV_WIDTH, ATTN_KV_WIDTH, RET_WIDTH, RET_WIDTH, RET_WIDTH, RET_WIDTH)
D_IN = sum(IN_SPLITS)

kernel_name = 'hybrid_swa_sink_retention_macaron'

def rms_norm(x, w):
    xf = x.astype(jnp.float32)
    y = xf * lax.rsqrt(jnp.mean(xf * xf, axis=-1, keepdims=True) + EPS)
    return (y * w.astype(jnp.float32)).astype(x.dtype)

def swiglu(h, w_gate, w_up, w_down):
    return (jax.nn.silu(h @ w_gate) * (h @ w_up)) @ w_down

def chunk_shift(t, j):
    if j == 0:
        return t
    return jnp.concatenate([jnp.zeros_like(t[:, :j]), t[:, :-j]], axis=1)

def sliding_window_sink_attention(q, k, v, sinks):
    b, s, hq, dh = q.shape
    hkv = k.shape[2]
    g = hq // hkv
    nc = s // CHUNK
    qc = q.reshape(b, nc, CHUNK, hkv, g, dh)
    kc = k.reshape(b, nc, CHUNK, hkv, dh)
    vc = v.reshape(b, nc, CHUNK, hkv, dh)
    offsets = list(range(WINDOW_CHUNKS - 1, -1, -1))
    kb = jnp.concatenate([chunk_shift(kc, j) for j in offsets], axis=2)
    vb = jnp.concatenate([chunk_shift(vc, j) for j in offsets], axis=2)
    chunk_idx = jnp.arange(nc)
    valid = jnp.concatenate(
        [jnp.broadcast_to((chunk_idx >= j)[:, None], (nc, CHUNK)) for j in offsets], axis=1)
    logits = jnp.einsum('bnqhgd,bnkhd->bnhgqk', qc, kb).astype(jnp.float32) * (dh ** -0.5)
    logits = jnp.where(valid[None, :, None, None, None, :], logits, -jnp.inf)
    sink = jnp.broadcast_to(sinks.astype(jnp.float32).reshape(hkv, g)[None, None, :, :, None, None],
                            logits.shape[:-1] + (1,))
    probs = jax.nn.softmax(jnp.concatenate([logits, sink], axis=-1), axis=-1)[..., :-1]
    out = jnp.einsum('bnhgqk,bnkhd->bnqhgd', probs.astype(v.dtype), vb)
    return out.reshape(b, s, hq * dh)

def rotary(t):
    s, d = t.shape[1], t.shape[-1]
    inv_freq = ROPE_BASE ** (-jnp.arange(0, d, 2, dtype=jnp.float32) / d)
    ang = jnp.arange(s, dtype=jnp.float32)[:, None] * inv_freq[None, :]
    cos, sin = jnp.cos(ang)[None, :, None, :], jnp.sin(ang)[None, :, None, :]
    t1, t2 = t[..., : d // 2], t[..., d // 2:]
    return jnp.concatenate([t1 * cos - t2 * sin, t1 * sin + t2 * cos], axis=-1)

def multiscale_retention(q, k, v):
    b, s, h, dk = q.shape
    dv = v.shape[-1]
    nc = s // CHUNK
    log_gamma = jnp.log(1.0 - 2.0 ** (-5.0 - jnp.arange(h, dtype=jnp.float32)))
    n = jnp.arange(CHUNK, dtype=jnp.float32)
    diff = n[:, None] - n[None, :]
    dmat = jnp.where(diff >= 0, jnp.exp(log_gamma[:, None, None] * jnp.maximum(diff, 0.0)), 0.0)
    xi = jnp.exp(log_gamma[:, None] * (n + 1.0))
    zeta = jnp.exp(log_gamma[:, None] * (CHUNK - 1.0 - n))
    gamma_c = jnp.exp(log_gamma * CHUNK)
    qc = q.reshape(b, nc, CHUNK, h, dk)
    kc = k.reshape(b, nc, CHUNK, h, dk)
    vc = v.reshape(b, nc, CHUNK, h, dv)
    scores = jnp.einsum('bnchd,bnmhd->bnhcm', qc, kc) * dmat[None, None]
    inner = jnp.einsum('bnhcm,bnmhe->bnche', scores, vc)
    qs = qc.transpose(1, 0, 3, 2, 4)
    ks = (kc.transpose(1, 0, 3, 2, 4)) * zeta[None, None, :, :, None]
    vs = vc.transpose(1, 0, 3, 2, 4)

    def step(state, inp):
        qi, ki, vi = inp
        cross = jnp.einsum('bhcd,bhde->bhce', qi, state) * xi[None, :, :, None]
        state = gamma_c[None, :, None, None] * state + jnp.einsum('bhcd,bhce->bhde', ki, vi)
        return state, cross

    state0 = jnp.zeros((b, h, dk, dv), jnp.float32)
    _, cross = lax.scan(step, state0, (qs, ks, vs))
    cross = cross.transpose(1, 0, 3, 2, 4)
    return (inner + cross).reshape(b, s, h, dv)

def head_group_mixer(h, w_in, attn_sinks, ret_gn_w, w_out):
    b, s, _ = h.shape
    p = h @ w_in
    bounds = list(np.cumsum(IN_SPLITS)[:-1])
    a_q, a_k, a_v, r_q, r_k, r_v, r_g = jnp.split(p, bounds, axis=-1)
    attn_out = sliding_window_sink_attention(
        a_q.reshape(b, s, ATTN_HEADS, ATTN_HEAD_DIM),
        a_k.reshape(b, s, ATTN_KV_HEADS, ATTN_HEAD_DIM),
        a_v.reshape(b, s, ATTN_KV_HEADS, ATTN_HEAD_DIM),
        attn_sinks)
    rq = rotary(r_q.astype(jnp.float32).reshape(b, s, RET_HEADS, RET_HEAD_DIM))
    rk = rotary(r_k.astype(jnp.float32).reshape(b, s, RET_HEADS, RET_HEAD_DIM)) * (RET_HEAD_DIM ** -0.5)
    rv = r_v.astype(jnp.float32).reshape(b, s, RET_HEADS, RET_HEAD_DIM)
    ro = multiscale_retention(rq, rk, rv)
    mu = jnp.mean(ro, axis=-1, keepdims=True)
    var = jnp.mean(jnp.square(ro - mu), axis=-1, keepdims=True)
    ro = ((ro - mu) * lax.rsqrt(var + EPS)).reshape(b, s, RET_WIDTH) * ret_gn_w.astype(jnp.float32)
    ret_out = (jax.nn.silu(r_g.astype(jnp.float32)) * ro).astype(h.dtype)
    return jnp.concatenate([attn_out, ret_out], axis=-1) @ w_out

def setup_inputs(seed: int = 0) -> dict:
    key = jax.random.key(seed)
    ks = jax.random.split(key, 16)

    def normal(k, shape, scale):
        return jax.random.normal(k, shape, jnp.float32) * scale

    return {
        'x': normal(ks[0], (BATCH, SEQ, D_MODEL), 1.0),
        'norm_ffn1_w': 1.0 + normal(ks[1], (DEPTH, D_MODEL), 0.02),
        'ffn1_w_gate': normal(ks[2], (DEPTH, D_MODEL, D_FF), D_MODEL ** -0.5),
        'ffn1_w_up': normal(ks[3], (DEPTH, D_MODEL, D_FF), D_MODEL ** -0.5),
        'ffn1_w_down': normal(ks[4], (DEPTH, D_FF, D_MODEL), D_FF ** -0.5),
        'norm_mix_w': 1.0 + normal(ks[5], (DEPTH, D_MODEL), 0.02),
        'w_in': normal(ks[6], (DEPTH, D_MODEL, D_IN), D_MODEL ** -0.5),
        'attn_sinks': normal(ks[7], (DEPTH, ATTN_HEADS), 1.0),
        'ret_gn_w': 1.0 + normal(ks[8], (DEPTH, RET_WIDTH), 0.02),
        'w_out': normal(ks[9], (DEPTH, D_MIX, D_MODEL), D_MIX ** -0.5),
        'norm_ffn2_w': 1.0 + normal(ks[10], (DEPTH, D_MODEL), 0.02),
        'ffn2_w_gate': normal(ks[11], (DEPTH, D_MODEL, D_FF), D_MODEL ** -0.5),
        'ffn2_w_up': normal(ks[12], (DEPTH, D_MODEL, D_FF), D_MODEL ** -0.5),
        'ffn2_w_down': normal(ks[13], (DEPTH, D_FF, D_MODEL), D_FF ** -0.5),
        'norm_final_w': 1.0 + normal(ks[14], (D_MODEL,), 0.02),
    }

def reference(x, norm_ffn1_w, ffn1_w_gate, ffn1_w_up, ffn1_w_down, norm_mix_w, w_in, attn_sinks,
              ret_gn_w, w_out, norm_ffn2_w, ffn2_w_gate, ffn2_w_up, ffn2_w_down, norm_final_w):
    for l in range(DEPTH):
        x = x + 0.5 * swiglu(rms_norm(x, norm_ffn1_w[l]), ffn1_w_gate[l], ffn1_w_up[l], ffn1_w_down[l])
        x = x + head_group_mixer(rms_norm(x, norm_mix_w[l]), w_in[l], attn_sinks[l], ret_gn_w[l], w_out[l])
        x = x + 0.5 * swiglu(rms_norm(x, norm_ffn2_w[l]), ffn2_w_gate[l], ffn2_w_up[l], ffn2_w_down[l])
    return rms_norm(x, norm_final_w)


_drawn_inputs = setup_inputs


def setup_inputs(seed=0):
    import zlib

    import numpy as np

    out = dict(_drawn_inputs(seed))
    spreads = {}
    factors = {'norm_ffn1_w': 5.322,
     'norm_mix_w': 3.399,
     'attn_sinks': 171.817,
     'ret_gn_w': 64.432,
     'norm_ffn2_w': 32.869,
     'norm_final_w': 21.64}
    for name, (base, spread) in spreads.items():
        noise = np.random.default_rng([zlib.crc32(name.encode()), seed]).standard_normal(out[name].shape)
        drawn = base * np.exp(spread * noise) if base else spread * noise
        out[name] = __import__('jax').numpy.asarray(drawn.astype(out[name].dtype))
    for name, factor in factors.items():
        out[name] = (out[name] * factor).astype(out[name].dtype)
    return out
```

```python
from contextlib import ExitStack

import numpy as np

import concourse.bass as bass
from concourse import mybir

P = 128
D = 2048
SEQ = 256
T = SEQ // P
KT = D // P
F = 5632
W = 512
NF = F // W
ND = D // W
D_IN = 5376
WI = 448
NI = D_IN // WI
CH = 64
HD = 64
KV = 2
QUAD = 4
NQ = 16 // QUAD
RH = 4
RD = 256
A_K, A_V, R_Q, R_V, R_G = 1024, 1152, 1280, 3328, 4352
EPS = 1e-6

RAW = 4
LEAD = 4
HALF = 2 * W

G_FFN = [0, 3 * NF + NI + 4]
G_IN = 3 * NF
G_OUT = G_IN + NI
HALVES = 8 * (G_FFN[1] + 3 * NF)
X_FFN = [2, 2 + 4 * NF + 8]
X_OUT = 2 + 4 * NF

FFN1, MIX, FFN2, FINAL = range(4)

ALU = mybir.AluOpType
ACT = mybir.ActivationFunctionType
AX = mybir.AxisListType
F32 = mybir.dt.float32
F32R = mybir.dt.float32r
BF16 = mybir.dt.bfloat16


def build(nc, x_d, norms_d, g1, u1, d1, w_in, sinks_d, gn_d, w_out, g2, u2, d2, fw_d, ident_d, cos_d, sin_d,
          decay_d, out_d):
    ffn_w = [(g1, u1, d1), (g2, u2, d2)]
    with ExitStack() as ctx:
        def sb(name, shape, dt=F32, stack=ctx):
            return stack.enter_context(nc.sbuf_tensor(name, shape, dt))

        def sem(name):
            return ctx.enter_context(nc.semaphore(name))

        x = sb("x", [P, T, D])
        xT_hi = sb("xT_hi", [P, KT, SEQ], F32R)
        xT_lo = sb("xT_lo", [P, KT, SEQ], F32R)
        raw = sb("raw", [P, RAW, 4 * W])
        w_hi = sb("w_hi", [P, LEAD, 2, W], F32R)
        w_lo = sb("w_lo", [P, LEAD, 2, W], F32R)
        proj = sb("proj", [P, T, D_IN])
        attT_hi = sb("attT_hi", [P, KT // 2, SEQ], F32R)
        attT_lo = sb("attT_lo", [P, KT // 2, SEQ], F32R)
        ident = sb("ident", [P, P])
        norms = sb("norms", [P, 3, KT])
        gn_w = sb("gn_w", [P, 8])
        sinks = sb("sinks", [P, NQ * T * QUAD])
        neg_sinks = sb("neg_sinks", [P, NQ * T * QUAD])
        cos = sb("cos", [P, T, RD // 2])
        sin = sb("sin", [P, T, RD // 2])
        decay = sb("decay", [P, RH, 3 * P])
        junk = sb("junk", [P, T, W], BF16)
        sq = sb("sq", [P, 4, T, ND])
        ms = sb("ms", [P, 4, T])
        ms_eps = sb("ms_eps", [P, 4, T])
        rstd = sb("rstd", [P, 4, T])
        minus_half = sb("minus_half", [P, T])
        with ExitStack() as ffn:
            sg = sb("sg", [P, T, W], F32, ffn)
            h = sb("h", [P, T, W], F32, ffn)
            hT_hi = sb("hT_hi", [P, 4, SEQ], F32R, ffn)
            hT_lo = sb("hT_lo", [P, 4, SEQ], F32R, ffn)
        q_in = sb("q_in", [P, T, QUAD * HD])
        qT_full = sb("qT", [P, T, QUAD * P])
        qT = qT_full[0:HD, :, :]
        kT_all = sb("kT_all", [HD, KV, T, 2, P])
        v_all = sb("v_all", [P, KV, T, 2, HD])
        kT = sb("kT", [HD, T, 2, P])
        v = sb("v", [P, T, 2, HD])
        probs = sb("probs", [P, T, QUAD, P])
        probsT = sb("probsT", [P, T, QUAD * P])
        att = sb("att", [P, T, QUAD * HD])
        lmax = sb("lmax", [P, T * QUAD])
        neg_m = sb("neg_m", [P, T * QUAD])
        sink_m = sb("sink_m", [P, T * QUAD])
        sink_e = sb("sink_e", [P, T * QUAD])
        den = sb("den", [P, T * QUAD])
        den2 = sb("den2", [P, T * QUAD])
        rden = sb("rden", [P, T * QUAD])
        rot_a = q_in[:].rearrange("p t (q c) -> p t q c", q=2)
        rot_b = qT_full[:, 0, :].rearrange("p (t q c) -> p t q c", t=T, q=2)
        rqT = probs[:].rearrange("p t h c -> p (t h c)")[:, 0:2 * SEQ].rearrange("p (k s) -> p k s", k=2)
        rkT = probs[:].rearrange("p t h c -> p (t h c)")[:, 2 * SEQ:4 * SEQ].rearrange("p (k s) -> p k s", k=2)
        scores = probsT[:, 0, 0:3 * P]
        y_raw = probsT[:, 1, :].rearrange("p (t c) -> p t c", t=T)
        y = att
        stats = sb("stats", [P, RH, T, 6])
        mv = sb("mv", [P, RH, T, 2])
        var_eps = sb("var_eps", [P, RH, T])
        gn_rstd = sb("gn_rstd", [P, RH, T])
        ps = ctx.enter_context(nc.psum_tensor("ps", [P, 8, W], F32))
        B_GATE, B_UP, B_DOWN = 0, 2, 4

        raw_loaded = [sem(f"raw_loaded{s}") for s in range(RAW)]
        x_loaded = [sem(f"x_loaded{n}") for n in range(ND)]
        consts_loaded = sem("consts_loaded")
        mix_consts = sem("mix_consts")
        fw_loaded = sem("fw_loaded")
        hi_ready = sem("hi_ready")
        lo_ready = sem("lo_ready")
        half_used = sem("half_used")
        xT_turned = sem("xT_turned")
        xT_hi_ready = sem("xT_hi_ready")
        xT_lo_ready = sem("xT_lo_ready")
        sq_ready = sem("sq_ready")
        ms_added = sem("ms_added")
        ms_ready = sem("ms_ready")
        rstd_ready = sem("rstd_ready")
        half_const = sem("half_const")
        silu_done = sem("silu_done")
        h_ready = sem("h_ready")
        hT_turned = sem("hT_turned")
        hT_hi_ready = sem("hT_hi_ready")
        hT_lo_ready = sem("hT_lo_ready")
        x_added = sem("x_added")
        proj_ready = sem("proj_ready")
        neg_sinks_ready = sem("neg_sinks_ready")
        k_turned = sem("k_turned")
        kT_ready = sem("kT_ready")
        kT_zeroed = sem("kT_zeroed")
        v_ready = sem("v_ready")
        q_in_ready = sem("q_in_ready")
        kT_in_ready = sem("kT_in_ready")
        v_in_ready = sem("v_in_ready")
        q_turned = sem("q_turned")
        qT_ready = sem("qT_ready")
        logits_ready = sem("logits_ready")
        soft = sem("soft")
        neg_m_ready = sem("neg_m_ready")
        sink_m_ready = sem("sink_m_ready")
        probs_ready = sem("probs_ready")
        sink_e_ready = sem("sink_e_ready")
        probs_turned = sem("probs_turned")
        probsT_a = sem("probsT_a")
        probsT_b = sem("probsT_b")
        pv_done = sem("pv_done")
        att_ready = sem("att_ready")
        att_turned = sem("att_turned")
        attT_hi_ready = sem("attT_hi_ready")
        attT_lo_ready = sem("attT_lo_ready")
        rot = sem("rot")
        gate_ready = sem("gate_ready")
        rqk_turned = sem("rqk_turned")
        rqT_ready = sem("rqT_ready")
        rkT_ready = sem("rkT_ready")
        scores_done = sem("scores_done")
        scores_ready = sem("scores_ready")
        ret_done = sem("ret_done")
        stats_done = sem("stats_done")
        mv_ready = sem("mv_ready")
        var_eps_ready = sem("var_eps_ready")
        gn_ready = sem("gn_ready")
        y_raw_ready = sem("y_raw_ready")
        y_ready = sem("y_ready")
        y_turned = sem("y_turned")
        retT_hi_ready = sem("retT_hi_ready")
        retT_lo_ready = sem("retT_lo_ready")
        out_ready = sem("out_ready")
        stored = sem("stored")

        block = ctx.enter_context(nc.Block())

        def f32(ap):
            return ap.bitcast(F32)

        def rot_view(half, head):
            qk = proj[:, :, R_Q:R_V].rearrange("p t (q h d) -> p t q h d", q=2, h=RH)
            return qk[:, :, :, head, half * (RD // 2):(half + 1) * (RD // 2)]

        @block.sync
        def _(sp):
            def load(g, s, src, width=W):
                if not (isinstance(g, int) and g == 0):
                    sp.wait_ge(lo_ready, 8 * g + 2 * s - 6)
                dst = raw[:, s, :].rearrange("p (k c) -> p k c", k=4)[:, :, 0:width]
                sp.dma_start(dst, src).then_inc(raw_loaded[s], 16)

            def rows(w, r0, c0, width=W):
                return w[bass.ds(r0, 4 * P), bass.ds(c0, width)].rearrange("(k p) c -> p k c", p=P)

            def load_ffn_in(f, g, i):
                for part in range(2):
                    for s in range(4):
                        load(g + part, s, rows(ffn_w[f][part], 4 * P * s, i * W))

            def load_ffn_down(f, g, i):
                for s in range(4):
                    load(g, s, rows(ffn_w[f][2], i * W, s * W))

            def load_ffn(f):
                load_ffn_in(f, G_FFN[f], 0)
                if f == 1:
                    sp.wait_ge(retT_lo_ready, RH)
                    sp.dma_start(proj[:, 0, 0:D], fw_d.partition_broadcast(P)).then_inc(fw_loaded, 16)
                with sp.Fori(1, NF) as i:
                    g = 3 * i + (G_FFN[f] - 1)
                    load_ffn_in(f, g, i)
                    load_ffn_down(f, g + 2, i - 1)
                load_ffn_down(f, G_FFN[f] + 3 * NF - 1, NF - 1)

            xv = x_d.rearrange("(t p) c -> p t c", p=P)
            sp.dma_start(ident[:], ident_d).then_inc(consts_loaded, 16)
            sp.dma_start(norms[:], norms_d).then_inc(consts_loaded, 16)
            for n in range(ND):
                sp.dma_start(x[:, :, n * W:(n + 1) * W], xv[:, :, n * W:(n + 1) * W]).then_inc(x_loaded[n], 16)
            for t, t_d in ((sinks, sinks_d), (gn_w, gn_d), (cos, cos_d), (sin, sin_d), (decay, decay_d)):
                sp.dma_start(t[:], t_d).then_inc(mix_consts, 16)
            load_ffn(0)
            with sp.Fori(0, NI) as b:
                for s in range(4):
                    load(b + G_IN, s, rows(w_in, 4 * P * s, b * WI, WI), WI)
            for part in range(2):
                for n in range(ND):
                    for u in range(2):
                        s = 2 * (n % 2) + u
                        load(G_OUT + 2 * part + n // 2, s, rows(w_out, D // 2 * part + 4 * P * u, n * W))
            load_ffn(1)
            ov = out_d.rearrange("(t p) c -> p t c", p=P)
            for t in range(T):
                for n in range(ND):
                    sp.wait_ge(out_ready, ND * t + n + 1)
                    sp.dma_start(ov[:, t, n * W:(n + 1) * W], x[:, t, n * W:(n + 1) * W]).then_inc(stored, 16)
            sp.wait_ge(stored, 16 * T * ND)

        @block.tensor
        def _(pe):
            def half(g, k, a_hi, a_lo, kt, bank, first, last, width=W):
                pe.wait_ge(lo_ready, 8 * g + (k + 1))
                for j in range(2):
                    for t in range(T):
                        out = ps[:, bank + t, 0:width]
                        xh, xl = (a[:, kt + j, t * P:(t + 1) * P] for a in (a_hi, a_lo))
                        wh, wl = (w[:, k % LEAD, j, 0:width] for w in (w_hi, w_lo))
                        pe.matmul(out, xh, wh, start=first and j == 0, stop=False)
                        pe.matmul(out, xh, wl, start=False, stop=False)
                        mm = pe.matmul(out, xl, wh, start=False, stop=last and j == 1)
                mm.then_inc(half_used, 1)

            def turn(bank, col, src):
                return pe.transpose(ps[0:src.shape[1], bank, col:col + P], src, ident[:])

            def turn_x(norm, n):
                if norm == FFN1:
                    pe.wait_ge(x_loaded[n], 16)
                else:
                    pe.wait_ge(x_added, {MIX: X_FFN[0] + 4 * (NF - 1), FFN2: X_OUT + 4}[norm] + n + 1)
                bank = (B_GATE, B_UP, B_DOWN, B_UP)[n]
                if n == 3:
                    pe.wait_ge(xT_lo_ready, 4 * norm + 2)
                elif n == 0 and norm == MIX:
                    pe.wait_ge(silu_done, T * NF)
                elif n == 1 and norm == MIX:
                    pe.wait_ge(h_ready, T * NF)
                elif n == 0 and norm == FFN2:
                    pe.wait_ge(rkT_ready, RH)
                    pe.wait_ge(rqT_ready, RH)
                elif n == 1 and norm == FFN2:
                    pe.wait_ge(retT_lo_ready, RH)
                    pe.wait_ge(y_raw_ready, T * RH)
                for j in range(4):
                    for t in range(T):
                        kt = 4 * n + j
                        mm = turn(bank + j // 2, (j % 2) * SEQ + t * P, x[:, t, kt * P:(kt + 1) * P])
                mm.then_inc(xT_turned, 1)

            def wide(norm, g, bank, width=W):
                for k in range(8):
                    if norm is not None and k % 2 == 0:
                        pe.wait_ge(xT_lo_ready, 4 * norm + k // 2 + 1)
                    half(g, k, xT_hi, xT_lo, 2 * k, bank, k == 0, k == 7, width)

            def turn_h(f, i):
                c = 11 * f + i
                pe.wait_ge(h_ready, 2 * c + 2)
                pe.wait_ge(x_added, 4 * i + (X_FFN[f] - 1))
                for b in range(2):
                    for j in range(2):
                        for t in range(T):
                            mm = turn(B_DOWN + b, j * SEQ + t * P, h[:, t, (2 * b + j) * P:(2 * b + j + 1) * P])
                    mm.then_inc(hT_turned, 1)

            def down(f, g, i, tail=False):
                c = 11 * f + i
                pe.wait_ge(hT_lo_ready, 2 * c + 2)
                for n in range(ND):
                    if n > 0:
                        pe.wait_ge(x_added, 4 * i + (X_FFN[f] + n - 1))
                    for u in range(2):
                        half(g, 2 * n + u, hT_hi, hT_lo, 2 * u, B_DOWN + 2 * (n % 2), u == 0, u == 1)
                    if tail and f == 0 and n in (1, 2):
                        turn_x(MIX, n - 1)
                if tail and f == 0:
                    turn_x(MIX, 2)
                    turn_x(MIX, 3)

            def ffn(f):
                norm = (FFN1, FFN2)[f]
                wide(norm, G_FFN[f], B_GATE)
                wide(norm, G_FFN[f] + 1, B_UP)
                with pe.Fori(1, NF) as i:
                    g = 3 * i + (G_FFN[f] - 1)
                    turn_h(f, i - 1)
                    pe.wait_ge(silu_done, 2 * i + 22 * f)
                    wide(None, g, B_GATE)
                    pe.wait_ge(h_ready, 2 * i + 22 * f)
                    wide(None, g + 1, B_UP)
                    down(f, g + 2, i - 1)
                turn_h(f, NF - 1)
                down(f, G_FFN[f] + 3 * NF - 1, NF - 1, tail=True)

            def logits(quad):
                pe.wait_ge(kT_ready, 3)
                pe.wait_ge(qT_ready, quad)
                pe.wait_ge(kT_in_ready, quad)
                for t in range(T):
                    for hh in range(QUAD):
                        for c in range(2):
                            n = CH if t == 0 and c == 0 else 2 * CH
                            mm = pe.matmul(ps[c * CH:(c + 1) * CH, B_DOWN + 2 + t, hh * P:hh * P + n],
                                           qT[:, t, hh * P + c * CH:hh * P + (c + 1) * CH],
                                           kT[:, t, c, 0:n], start=True, stop=True)
                mm.then_inc(logits_ready, 1)

            def weigh(quad):
                pe.wait_ge(probsT_a, quad)
                pe.wait_ge(probsT_b, quad)
                pe.wait_ge(v_in_ready, quad)
                for t in range(T):
                    for hh in range(QUAD):
                        for c in range(2):
                            col = (t * QUAD + hh) * HD
                            mm = pe.matmul(ps[c * CH:(c + 1) * CH, B_DOWN + 2, col:col + HD],
                                           probsT[:, t, hh * P + c * CH:hh * P + (c + 1) * CH],
                                           v[:, t, c, :], start=True, stop=True)
                mm.then_inc(pv_done, 1)

            def in_projection():
                def pair(i, quad=None):
                    if quad is not None:
                        pe.wait_ge(kT_ready, 3)
                        pe.wait_ge(q_in_ready, quad)
                        for t in range(T):
                            for hh in range(QUAD):
                                mm = turn(B_DOWN + t, hh * P, q_in[:, t, hh * HD:(hh + 1) * HD])
                        mm.then_inc(q_turned, 1)
                    for e in range(2):
                        pe.wait_ge(proj_ready, 2 * i + (e + 1))
                        for k in range(8):
                            if quad is None and k % 2 == 0:
                                pe.wait_ge(xT_lo_ready, 4 * MIX + k // 2 + 1)
                            if quad is not None and (e, k) == (0, 1):
                                pe.wait_ge(attT_lo_ready, quad)
                            half(2 * i + (G_IN + e), k, xT_hi, xT_lo, 2 * k, B_GATE + 2 * e, k == 0, k == 7, WI)
                            if quad is not None and (e, k) == (0, 1):
                                logits(quad)
                            if quad is not None and (e, k) == (0, 6):
                                pe.wait_ge(probs_ready, quad)
                                for t in range(T):
                                    for hh in range(QUAD):
                                        mm = turn(B_DOWN + t, hh * P, probs[:, t, hh, :])
                                mm.then_inc(probs_turned, 1)
                            if quad is not None and (e, k) == (1, 1):
                                weigh(quad)
                            if quad is not None and (e, k) == (1, 4):
                                pe.wait_ge(att_ready, quad)
                                for k2 in range(2):
                                    for t in range(T):
                                        mm = turn(B_DOWN + 3, k2 * SEQ + t * P, att[:, t, k2 * P:(k2 + 1) * P])
                                mm.then_inc(att_turned, 1)

                with pe.Fori(0, 2) as i:
                    pair(i)
                pe.wait_ge(proj_ready, 2 + 3)
                for g in range(KV):
                    for t in range(T):
                        mm = turn(B_DOWN, (g * T + t) * P, proj[:, t, A_K + g * HD:A_K + (g + 1) * HD])
                mm.then_inc(k_turned, 1)
                pe.wait_ge(kT_ready, 3)
                with pe.Fori(1, NQ + 1) as quad:
                    pair(quad + 1, quad)

            def retention_start(hd):
                pe.wait_ge(rot, 6 * (hd + 1))
                pe.wait_ge(proj_ready, 2 + NI)
                if hd:
                    pe.wait_ge(rqT_ready, hd)
                    pe.wait_ge(rkT_ready, hd)
                for qk in range(2):
                    for dt in range(2):
                        for t in range(T):
                            c0 = R_Q + qk * RH * RD + hd * RD + dt * P
                            mm = turn(B_GATE + qk, dt * SEQ + t * P, proj[:, t, c0:c0 + P])
                mm.then_inc(rqk_turned, 1)

            def retention_scores(hd):
                pe.wait_ge(rqT_ready, hd + 1)
                pe.wait_ge(rkT_ready, hd + 1)
                if hd:
                    pe.wait_ge(retT_lo_ready, hd)
                for m in range(T):
                    for dt in range(2):
                        mm = pe.matmul(ps[:, B_UP, 2 * P * m:2 * P * m + SEQ - m * P], rkT[:, dt, m * P:(m + 1) * P],
                                       rqT[:, dt, m * P:SEQ], start=dt == 0, stop=dt == 1)
                mm.then_inc(scores_done, 1)

            def retention_out(hd):
                pe.wait_ge(scores_ready, hd + 1)
                if hd:
                    pe.wait_ge(y_raw_ready, T * hd)
                for t in range(T):
                    for m in range(t + 1):
                        c0 = 2 * P * m + (t - m) * P
                        mm = pe.matmul(ps[:, B_UP + 1, t * RD:(t + 1) * RD], scores[:, c0:c0 + P],
                                       proj[:, m, R_V + hd * RD:R_V + (hd + 1) * RD], start=m == 0, stop=m == t)
                mm.then_inc(ret_done, 1)

            def retention_turn(hd):
                pe.wait_ge(y_ready, hd + 1)
                for k2 in range(2):
                    for t in range(T):
                        mm = turn(B_UP, k2 * SEQ + t * P, y[:, t, k2 * P:(k2 + 1) * P])
                mm.then_inc(y_turned, 1)

            for n in range(ND):
                if n == 0:
                    pe.wait_ge(consts_loaded, 32)
                turn_x(FFN1, n)
            ffn(0)
            in_projection()
            pe.wait_ge(attT_lo_ready, 1 + NQ)
            for n in range(ND):
                retention_start(n)
                if n >= 2:
                    pe.wait_ge(x_added, X_OUT + n - 1)
                for k in range(4):
                    half(G_OUT, 4 * n + k, attT_hi, attT_lo, 2 * k, B_DOWN + 2 * (n % 2), k == 0, k == 3)
                    if k == 0:
                        retention_scores(n)
                    if k == 1:
                        retention_out(n)
                retention_turn(n)
            pe.wait_ge(retT_lo_ready, RH)
            for n in range(ND):
                pe.wait_ge(x_added, X_OUT + 4 + n - 1)
                for k in range(4):
                    half(G_OUT + 2, 4 * n + k, xT_hi, xT_lo, 8 + 2 * k, B_DOWN + 2 * (n % 2), k == 0, k == 3)
                    if k == 1 and n in (1, 2):
                        turn_x(FFN2, n - 1)
            turn_x(FFN2, 2)
            turn_x(FFN2, 3)
            ffn(1)

        @block.scalar
        def _(act):
            def split(g, k, first=False):
                g, k = g + k // 8, k % 8
                s = k // 2
                if not first:
                    act.wait_ge(half_used, 8 * g + (k + 1 - LEAD))
                if k % 2 == 0:
                    act.wait_ge(raw_loaded[s], 16 * g + 16)
                dst = w_hi[:, k % LEAD, :, :].rearrange("p k c -> p (k c)")
                act.activation(dst, raw[:, s, (k % 2) * HALF:(k % 2 + 1) * HALF], ACT.Copy).then_inc(hi_ready, 1)

            def position(g, k):
                if not (isinstance(g, int) and 8 * g + k + LEAD >= HALVES):
                    split(g, k + LEAD)

            def xT(norm, n):
                act.wait_ge(xT_turned, 4 * norm + n + 1)
                bank = (B_GATE, B_UP, B_DOWN, B_UP)[n]
                for j in range(4):
                    kt = 4 * n + j
                    a = act.activation(xT_hi[:, kt, :], ps[:, bank + j // 2, (j % 2) * SEQ:(j % 2 + 1) * SEQ],
                                       ACT.Copy, scale=norms[:, norm, kt:kt + 1])
                a.then_inc(xT_hi_ready, 1)

            def squares(norm, n):
                if norm == FFN1:
                    act.wait_ge(x_loaded[n], 16)
                else:
                    act.wait_ge(x_added, {MIX: X_FFN[0] + 4 * (NF - 1), FFN2: X_OUT + 4,
                                          FINAL: X_FFN[1] + 4 * (NF - 1)}[norm] + n + 1)
                for t in range(T):
                    c = T * (4 * norm + n) + t
                    if c >= T:
                        act.wait_ge(sq_ready, c - T + 1)
                    act.activation(junk[:, t, :], x[:, t, n * W:(n + 1) * W], ACT.Square,
                                   accum_out=sq[:, norm, t, n:n + 1]).then_inc(sq_ready, 1)

            def silu(f, g, i):
                act.wait_ge(half_used, 8 * g + 8)
                for t in range(T):
                    if not (isinstance(i, int) and f == 0):
                        act.wait_ge(h_ready, 2 * i + (22 * f + t - 1))
                    act.activation(sg[:, t, :], ps[:, B_GATE + t, :], ACT.Silu,
                                   scale=rstd[:, (FFN1, FFN2)[f], t:t + 1]).then_inc(silu_done, 1)

            def hT(f, i):
                for b in range(2):
                    act.wait_ge(hT_turned, 2 * i + (22 * f + b + 1))
                    act.activation(hT_hi[:, 2 * b:2 * b + 2, :].rearrange("p k s -> p (k s)"), ps[:, B_DOWN + b, :],
                                   ACT.Copy).then_inc(hT_hi_ready, 1)

            def ffn(f):
                g0 = G_FFN[f]
                for k in range(16):
                    position(g0, k)
                    if k == 7:
                        act.wait_ge(rstd_ready, (FFN1, FFN2)[f] + 1)
                        silu(f, g0, 0)
                with act.Fori(1, NF) as i:
                    g = 3 * i + (g0 - 1)
                    for k in range(24):
                        position(g, k)
                        if k == 0:
                            hT(f, i - 1)
                        if k == 7:
                            silu(f, g, i)
                g = g0 + 3 * NF - 1
                hT(f, NF - 1)
                for k in range(8):
                    position(g, k)
                    if f == 0:
                        if k in (3, 5):
                            xT(MIX, (k - 3) // 2)
                            squares(MIX, (k - 3) // 2)
                        if k == 7:
                            for n in (2, 3):
                                xT(MIX, n)
                            for n in (2, 3):
                                squares(MIX, n)
                    elif k % 2:
                        squares(FINAL, k // 2)

            def proj_out(b, bank):
                act.wait_ge(half_used, 8 * b + (8 * G_IN + 8))
                for t in range(T):
                    a = act.activation(proj[:, t, bass.ds(b * WI, WI)], ps[:, bank + t, 0:WI], ACT.Copy,
                                       scale=rstd[:, MIX, t:t + 1])
                a.then_inc(proj_ready, 1)

            def in_pair(i, j=None):
                for k in range(16):
                    position(2 * i + G_IN, k)
                    if k == 7:
                        proj_out(2 * i, B_GATE)
                    if k == 15:
                        proj_out(2 * i + 1, B_UP)
                    if j is None:
                        continue
                    if k == 0:
                        act.wait_ge(q_turned, j + 1)
                        act.activation(qT.rearrange("p t c -> p (t c)"),
                                       ps[0:HD, B_DOWN:B_DOWN + 2, :].rearrange("p t c -> p (t c)"),
                                       ACT.Copy).then_inc(qT_ready, 1)
                    if k == 2:
                        act.wait_ge(neg_m_ready, j + 1)
                        for t in range(T):
                            for hh in range(QUAD):
                                c = t * QUAD + hh
                                a = act.activation(probs[:, t, hh, :], ps[:, B_DOWN + 2 + t, hh * P:(hh + 1) * P],
                                                   ACT.Exp, bias=neg_m[:, c:c + 1], scale=HD ** -0.5,
                                                   accum_out=den[:, c:c + 1])
                        a.then_inc(probs_ready, 1)
                        act.wait_ge(sink_m_ready, j + 1)
                        act.activation(sink_e[:], sink_m[:], ACT.Exp).then_inc(sink_e_ready, 1)
                    if k == 6:
                        act.wait_ge(probs_turned, j + 1)
                        act.activation(probsT[:, 0, :], ps[:, B_DOWN, :], ACT.Copy).then_inc(probsT_a, 1)
                    if k == 12:
                        act.wait_ge(att_turned, j + 1)
                        act.activation(attT_hi[:, bass.ds(2 * j, 2), :], ps[:, B_DOWN + 3, :].rearrange(
                            "p (k s) -> p k s", k=2), ACT.Copy).then_inc(attT_hi_ready, 1)

            act.wait_ge(consts_loaded, 32)
            for n in range(ND):
                xT(FFN1, n)
                squares(FFN1, n)
                split(0, n, first=True)
            ffn(0)
            act.sem_inc(proj_ready, 2)
            act.wait_ge(rstd_ready, MIX + 1)
            with act.Fori(0, 2) as i:
                in_pair(i)
            with act.Fori(0, NQ) as j:
                in_pair(j + 2, j)
            for n in range(ND):
                for k in range(4):
                    position(G_OUT, 4 * n + k)
                    if k == 0:
                        act.wait_ge(rqk_turned, n + 1)
                        act.activation(rqT.rearrange("p k s -> p (k s)"), ps[:, B_GATE, :],
                                       ACT.Copy).then_inc(rqT_ready, 1)
                        gate = proj[:, :, R_G + n * RD:R_G + (n + 1) * RD]
                        if n == 0:
                            act.wait_ge(proj_ready, 2 + NI)
                        act.activation(gate, gate, ACT.Silu).then_inc(gate_ready, 1)
                    if k == 2:
                        act.wait_ge(gn_ready, n + 1)
                        act.wait_ge(y_raw_ready, T * (n + 1))
                        if n:
                            act.wait_ge(y_turned, n)
                        for t in range(T):
                            a = act.activation(y[:, t, :], y_raw[:, t, :], ACT.Copy, scale=gn_rstd[:, n, t:t + 1])
                        a.then_inc(y_ready, 1)
                    if k == 3:
                        act.wait_ge(y_turned, n + 1)
                        for k2 in range(2):
                            a = act.activation(xT_hi[:, 8 + 2 * n + k2, :], ps[:, B_UP, k2 * SEQ:(k2 + 1) * SEQ],
                                               ACT.Copy, scale=gn_w[:, 2 * n + k2:2 * n + k2 + 1])
                        a.then_inc(retT_hi_ready, 1)
            for k in range(16):
                position(G_OUT + 2, k)
                if k in (6, 10):
                    xT(FFN2, (k - 6) // 4)
                    squares(FFN2, (k - 6) // 4)
                if k == 15:
                    for n in (2, 3):
                        xT(FFN2, n)
                    for n in (2, 3):
                        squares(FFN2, n)
            ffn(1)

        @block.vector
        def _(dve):
            def split(g, k):
                g, k = g + k // 8, k % 8
                dve.wait_ge(hi_ready, 8 * g + (k + 1))
                flat = "p k c -> p (k c)"
                dve.tensor_tensor(w_lo[:, k % LEAD, :, :].rearrange(flat),
                                  raw[:, k // 2, (k % 2) * HALF:(k % 2 + 1) * HALF],
                                  f32(w_hi[:, k % LEAD, :, :].rearrange(flat)), ALU.subtract).then_inc(lo_ready, 1)

            def position(g, k):
                if not (isinstance(g, int) and 8 * g + k + LEAD >= HALVES):
                    split(g, k + LEAD)

            def xT(norm, n):
                dve.wait_ge(xT_hi_ready, 4 * norm + n + 1)
                bank = (B_GATE, B_UP, B_DOWN, B_UP)[n]
                for j in range(4):
                    kt = 4 * n + j
                    a = dve.scalar_tensor_tensor(out=xT_lo[:, kt, :],
                                                 in0=ps[:, bank + j // 2, (j % 2) * SEQ:(j % 2 + 1) * SEQ],
                                                 scalar=norms[:, norm, kt:kt + 1], in1=f32(xT_hi[:, kt, :]),
                                                 op0=ALU.mult, op1=ALU.subtract)
                a.then_inc(xT_lo_ready, 1)

            def mean_square(norm):
                dve.wait_ge(sq_ready, T * (4 * norm + 4))
                dve.tensor_reduce(ms[:, norm, :], sq[:, norm, :, :], AX.X, ALU.add).then_inc(ms_added, 1)
                dve.wait_ge(ms_added, norm + 1)
                dve.tensor_scalar(ms_eps[:, norm, :], ms[:, norm, :], 1.0 / D, EPS, ALU.mult,
                                  ALU.add).then_inc(ms_ready, 1)

            def gated(f, g, i):
                dve.wait_ge(half_used, 8 * g + 16)
                for t in range(T):
                    dve.wait_ge(silu_done, 2 * i + (22 * f + t + 1))
                    if not (isinstance(i, int) and f == 0) and t == 0:
                        dve.wait_ge(hT_turned, 2 * i + 22 * f)
                    dve.scalar_tensor_tensor(out=h[:, t, :], in0=ps[:, B_UP + t, :],
                                             scalar=rstd[:, (FFN1, FFN2)[f], t:t + 1], in1=sg[:, t, :],
                                             op0=ALU.mult, op1=ALU.mult).then_inc(h_ready, 1)

            def hT(f, i):
                for b in range(2):
                    dve.wait_ge(hT_hi_ready, 2 * i + (22 * f + b + 1))
                    dve.tensor_tensor(hT_lo[:, 2 * b:2 * b + 2, :].rearrange("p k s -> p (k s)"),
                                      ps[:, B_DOWN + b, :],
                                      f32(hT_hi[:, 2 * b:2 * b + 2, :].rearrange("p k s -> p (k s)")),
                                      ALU.subtract).then_inc(hT_lo_ready, 1)

            def add(g, k, n, scale):
                dve.wait_ge(half_used, 8 * g + (k + 1))
                for t in range(T):
                    xb = x[:, t, n * W:(n + 1) * W]
                    a = dve.scalar_tensor_tensor(out=xb, in0=ps[:, B_DOWN + 2 * (n % 2) + t, :], scalar=scale,
                                                 in1=xb, op0=ALU.mult, op1=ALU.add)
                a.then_inc(x_added, 1)

            def ffn(f):
                g0 = G_FFN[f]
                for k in range(16):
                    position(g0, k)
                    if k == 15:
                        dve.wait_ge(rstd_ready, (FFN1, FFN2)[f] + 1)
                        gated(f, g0, 0)
                with dve.Fori(1, NF) as i:
                    g = 3 * i + (g0 - 1)
                    for k in range(24):
                        position(g, k)
                        if k == 0:
                            hT(f, i - 1)
                        if k == 15:
                            gated(f, g, i)
                        if k >= 16 and k % 2:
                            add(g, k, (k - 16) // 2, 0.5)
                g = g0 + 3 * NF - 1
                hT(f, NF - 1)
                for k in range(8):
                    position(g, k)
                    if k % 2:
                        add(g, k, k // 2, 0.5)
                    if f == 0 and k in (3, 5):
                        xT(MIX, (k - 3) // 2)
                    if f == 0 and k == 7:
                        xT(MIX, 2)
                        xT(MIX, 3)
                        mean_square(MIX)

            def in_pair(i, j=None):
                for k in range(16):
                    position(2 * i + G_IN, k)
                    if j is None:
                        continue
                    if k == 1:
                        dve.wait_ge(logits_ready, j + 1)
                        first = ps[0:CH, B_DOWN + 2, :].rearrange("p (h c) -> p h c", h=QUAD)
                        dve.memset(first[:, :, CH:2 * CH], -3.0e38).then_inc(soft, 1)
                        dve.wait_ge(soft, 4 * j + 1)
                        dve.tensor_reduce(lmax[:], ps[:, B_DOWN + 2:B_DOWN + 4, :].rearrange(
                            "p t (h c) -> p (t h) c", h=QUAD), AX.X, ALU.max).then_inc(soft, 1)
                        dve.wait_ge(soft, 4 * j + 2)
                        dve.scalar_tensor_tensor(out=neg_m[:], in0=lmax[:], scalar=-HD ** -0.5,
                                                 in1=neg_sinks[:, bass.ds(8 * j, 8)], op0=ALU.mult,
                                                 op1=ALU.min).then_inc(neg_m_ready, 1)
                        dve.wait_ge(neg_m_ready, j + 1)
                        dve.tensor_tensor(sink_m[:], sinks[:, bass.ds(8 * j, 8)], neg_m[:],
                                          ALU.add).then_inc(sink_m_ready, 1)
                    if k == 6:
                        dve.wait_ge(sink_e_ready, j + 1)
                        dve.tensor_tensor(den2[:], den[:], sink_e[:], ALU.add).then_inc(soft, 1)
                        dve.wait_ge(soft, 4 * j + 3)
                        dve.reciprocal(rden[:], den2[:]).then_inc(soft, 1)
                        dve.wait_ge(probs_turned, j + 1)
                        dve.tensor_copy(probsT[:, 1, :], ps[:, B_DOWN + 1, :]).then_inc(probsT_b, 1)
                    if k == 9:
                        dve.wait_ge(pv_done, j + 1)
                        dve.wait_ge(soft, 4 * j + 4)
                        dve.tensor_tensor(att[:].rearrange("p t (h d) -> p (t h) d", h=QUAD),
                                          ps[:, B_DOWN + 2, :].rearrange("p (h d) -> p h d", d=HD),
                                          rden[:].unsqueeze(2).to_broadcast([P, T * QUAD, HD]),
                                          ALU.mult).then_inc(att_ready, 1)
                    if k == 12:
                        dve.wait_ge(attT_hi_ready, j + 1)
                        dve.tensor_tensor(attT_lo[:, bass.ds(2 * j, 2), :],
                                          ps[:, B_DOWN + 3, :].rearrange("p (k s) -> p k s", k=2),
                                          f32(attT_hi[:, bass.ds(2 * j, 2), :]),
                                          ALU.subtract).then_inc(attT_lo_ready, 1)

            dve.sem_inc(x_added, X_FFN[0])
            dve.sem_inc(attT_lo_ready, 1)
            dve.wait_ge(mix_consts, 16 * 5)
            dve.tensor_scalar(neg_sinks[:], sinks[:], -1.0, None, ALU.mult).then_inc(neg_sinks_ready, 1)
            dve.wait_ge(consts_loaded, 32)
            for n in range(ND):
                xT(FFN1, n)
                split(0, n)
            mean_square(FFN1)
            ffn(0)
            with dve.Fori(0, 2) as i:
                in_pair(i)
            dve.wait_ge(k_turned, 1)
            dve.wait_ge(kT_zeroed, 1)
            turned = ps[0:HD, B_DOWN, :].rearrange("p (g t c) -> p g t c", g=KV, t=T)
            dve.tensor_copy(kT_all[:, :, :, 1, :], turned).then_inc(kT_ready, 1)
            dve.tensor_copy(kT_all[:, :, :, 0, 0:CH], turned[:, :, :, 0:CH]).then_inc(kT_ready, 1)
            dve.tensor_copy(kT_all[:, :, 1, 0, CH:2 * CH], turned[:, :, 0, CH:2 * CH]).then_inc(kT_ready, 1)
            dve.wait_ge(neg_sinks_ready, 1)
            with dve.Fori(0, NQ) as j:
                in_pair(j + 2, j)
            for n in range(ND):
                for k in range(4):
                    position(G_OUT, 4 * n + k)
                    if k == 0:
                        dve.wait_ge(rqk_turned, n + 1)
                        dve.tensor_copy(rkT.rearrange("p k s -> p (k s)"),
                                        ps[:, B_GATE + 1, :]).then_inc(rkT_ready, 1)
                        dve.wait_ge(scores_done, n + 1)
                        dve.tensor_tensor(scores, ps[:, B_UP, 0:3 * P], decay[:, n, :],
                                          ALU.mult).then_inc(scores_ready, 1)
                    if k == 1:
                        dve.wait_ge(ret_done, n + 1)
                        for t in range(T):
                            dve.bn_stats(stats[:, n, t, :], ps[:, B_UP + 1, t * RD:(t + 1) * RD]).then_inc(stats_done, 1)
                        for t in range(T):
                            dve.wait_ge(stats_done, T * n + t + 1)
                            dve.bn_aggr(mv[:, n, t, :], stats[:, n, t, :]).then_inc(mv_ready, 1)
                        dve.wait_ge(gate_ready, n + 1)
                        dve.wait_ge(mv_ready, T * (n + 1))
                        if n:
                            dve.wait_ge(y_ready, n)
                        for t in range(T):
                            dve.scalar_tensor_tensor(out=y_raw[:, t, :], in0=ps[:, B_UP + 1, t * RD:(t + 1) * RD],
                                                     scalar=mv[:, n, t, 0:1],
                                                     in1=proj[:, t, R_G + n * RD:R_G + (n + 1) * RD],
                                                     op0=ALU.subtract, op1=ALU.mult).then_inc(y_raw_ready, 1)
                    if k == 3:
                        dve.wait_ge(retT_hi_ready, n + 1)
                        for k2 in range(2):
                            a = dve.scalar_tensor_tensor(
                                out=xT_lo[:, 8 + 2 * n + k2, :], in0=ps[:, B_UP, k2 * SEQ:(k2 + 1) * SEQ],
                                scalar=gn_w[:, 2 * n + k2:2 * n + k2 + 1], in1=f32(xT_hi[:, 8 + 2 * n + k2, :]),
                                op0=ALU.mult, op1=ALU.subtract)
                        a.then_inc(retT_lo_ready, 1)
                        add(G_OUT, 4 * n + 3, n, 1.0)
            for k in range(16):
                position(G_OUT + 2, k)
                if k % 4 == 3:
                    add(G_OUT + 2, k, k // 4, 1.0)
                if k in (6, 10):
                    xT(FFN2, (k - 6) // 4)
            xT(FFN2, 2)
            xT(FFN2, 3)
            mean_square(FFN2)
            ffn(1)
            mean_square(FINAL)
            dve.wait_ge(rstd_ready, FINAL + 1)
            dve.wait_ge(fw_loaded, 16)
            for t in range(T):
                for n in range(ND):
                    xb = x[:, t, n * W:(n + 1) * W]
                    dve.scalar_tensor_tensor(out=xb, in0=xb, scalar=rstd[:, FINAL, t:t + 1],
                                             in1=proj[:, 0, n * W:(n + 1) * W], op0=ALU.mult,
                                             op1=ALU.mult).then_inc(out_ready, 1)

        @block.gpsimd
        def _(pool):
            def rsqrt_of_norm(norm):
                pool.wait_ge(ms_ready, norm + 1)
                pool.tensor_tensor(rstd[:, norm, :], ms_eps[:, norm, :], minus_half[:],
                                   ALU.pow).then_inc(rstd_ready, 1)

            def stage(j):
                again = not isinstance(j, int)
                if again:
                    pool.wait_ge(q_turned, j)
                    pool.wait_ge(v_in_ready, j)
                pool.tensor_copy(q_in[:], proj[:, :, bass.ds(j * QUAD * HD, QUAD * HD)]).then_inc(q_in_ready, 1)
                if again:
                    pool.wait_ge(logits_ready, j)
                pool.wait_ge(q_in_ready, j + 1)
                pool.tensor_copy(kT[:], kT_all[:, bass.ds(j // 2, 1), :, :, :].rearrange(
                    "p g t v c -> p (g t) v c")).then_inc(kT_in_ready, 1)
                if again:
                    pool.wait_ge(pv_done, j)
                pool.wait_ge(kT_in_ready, j + 1)
                pool.tensor_copy(v[:], v_all[:, bass.ds(j // 2, 1), :, :, :].rearrange(
                    "p g t v c -> p (g t) v c")).then_inc(v_in_ready, 1)

            def rotate(hd):
                t1, t2 = rot_view(0, hd), rot_view(1, hd)
                c, s = (a[:].unsqueeze(2).to_broadcast([P, T, 2, RD // 2]) for a in (cos, sin))
                step = 6 * hd
                if hd:
                    pool.wait_ge(rot, step)
                pool.tensor_tensor(rot_a, t1, s, ALU.mult).then_inc(rot, 1)
                pool.tensor_tensor(rot_b, t2, s, ALU.mult).then_inc(rot, 1)
                pool.wait_ge(rot, step + 2)
                pool.tensor_tensor(t1, t1, c, ALU.mult).then_inc(rot, 1)
                pool.tensor_tensor(t2, t2, c, ALU.mult).then_inc(rot, 1)
                pool.wait_ge(rot, step + 4)
                pool.tensor_tensor(t1, t1, rot_b, ALU.subtract).then_inc(rot, 1)
                pool.tensor_tensor(t2, t2, rot_a, ALU.add).then_inc(rot, 1)

            def rsqrt_of_head(hd):
                pool.wait_ge(mv_ready, T * (hd + 1))
                pool.tensor_scalar(var_eps[:, hd, :], mv[:, hd, :, 1], EPS, None, ALU.add).then_inc(var_eps_ready, 1)
                pool.wait_ge(var_eps_ready, hd + 1)
                pool.tensor_tensor(gn_rstd[:, hd, :], var_eps[:, hd, :], minus_half[:], ALU.pow).then_inc(gn_ready, 1)

            pool.memset(minus_half[:], -0.5).then_inc(half_const, 1)
            pool.wait_ge(half_const, 1)
            rsqrt_of_norm(FFN1)
            rsqrt_of_norm(MIX)
            pool.wait_ge(rstd_ready, MIX + 1)
            pool.memset(kT_all[:, :, 0, 0, CH:2 * CH], 0.0).then_inc(kT_zeroed, 1)
            pool.wait_ge(kT_zeroed, 1)
            pool.memset(v_all[CH:P, :, 0, 0, :], 0.0).then_inc(v_ready, 1)
            pool.wait_ge(proj_ready, 2 + 3)
            pool.wait_ge(v_ready, 1)
            vals = proj[:, :, A_V:R_Q].rearrange("p t (g d) -> p g t d", g=KV)
            pool.tensor_copy(v_all[:, :, :, 1, :], vals).then_inc(v_ready, 1)
            pool.wait_ge(v_ready, 2)
            pool.tensor_copy(v_all[0:CH, :, :, 0, :], vals[0:CH]).then_inc(v_ready, 1)
            pool.wait_ge(v_ready, 3)
            pool.tensor_copy(v_all[CH:P, :, 1, 0, :], vals[CH:P, :, 0, :]).then_inc(v_ready, 1)
            pool.wait_ge(kT_ready, 3)
            pool.wait_ge(v_ready, 4)
            stage(0)
            with pool.Fori(1, NQ) as j:
                stage(j)
            pool.wait_ge(v_in_ready, NQ)
            pool.wait_ge(proj_ready, 2 + 8)
            pool.wait_ge(mix_consts, 16 * 5)
            pool.wait_ge(logits_ready, NQ)
            for hd in range(RH):
                rotate(hd)
            for hd in range(RH):
                rsqrt_of_head(hd)
            rsqrt_of_norm(FFN2)
            rsqrt_of_norm(FINAL)


def constants():
    inv = np.float32(10000.0) ** (-np.arange(0, RD, 2, dtype=np.float32) / np.float32(RD))
    ang = np.arange(SEQ, dtype=np.float32)[:, None] * inv.astype(np.float32)[None, :]
    by_token = [f(ang).astype(np.float32).reshape(T, P, RD // 2).transpose(1, 0, 2) for f in (np.cos, np.sin)]
    log_gamma = np.log(1.0 - 2.0 ** (-5.0 - np.arange(RH, dtype=np.float64)))
    n = np.arange(SEQ)
    dist = n[None, :] - n[:, None]
    full = np.where(dist >= 0, np.exp(log_gamma[:, None, None] * np.maximum(dist, 0)), 0.0) * RD ** -0.5
    tiles = np.concatenate([full[:, 0:P, :], full[:, P:SEQ, P:SEQ]], axis=2)
    return {"ident": np.eye(P, dtype=np.float32), "cos": by_token[0], "sin": by_token[1],
            "decay": tiles.transpose(1, 0, 2).astype(np.float32)}


def kernel(**inputs):
    import concourse.bacc as bacc
    from concourse.bass_utils import run_bass_kernel_spmd

    a = {k: np.asarray(v) for k, v in inputs.items()}

    def by_feature(w, n):
        return w.reshape(n, P).T

    arrays = {
        "x": a["x"].reshape(SEQ, D),
        "norms": np.stack([by_feature(a[k], KT) for k in ("norm_ffn1_w", "norm_mix_w", "norm_ffn2_w")], axis=1),
        "g1": a["ffn1_w_gate"][0], "u1": a["ffn1_w_up"][0], "d1": a["ffn1_w_down"][0],
        "w_in": a["w_in"][0],
        "sinks": np.broadcast_to(a["attn_sinks"].reshape(1, NQ, 1, QUAD), (P, NQ, T, QUAD)).reshape(P, -1),
        "gn": by_feature(a["ret_gn_w"], 8),
        "w_out": a["w_out"][0],
        "g2": a["ffn2_w_gate"][0], "u2": a["ffn2_w_up"][0], "d2": a["ffn2_w_down"][0],
        "fw": a["norm_final_w"],
        **constants(),
    }
    nc = bacc.Bacc("TRN2", target_bir_lowering=False, num_devices=1)
    feed, args = {}, []
    for name, arr in arrays.items():
        arr = np.ascontiguousarray(arr)
        feed[f"in_{name}"] = arr
        args.append(nc.dram_tensor(f"in_{name}", arr.shape, mybir.dt.from_np(arr.dtype), kind="ExternalInput").ap())
    out = nc.dram_tensor("out", (SEQ, D), F32, kind="ExternalOutput").ap()
    build(nc, *args, out)
    r = run_bass_kernel_spmd(nc, [feed], core_ids=[0])
    return r.results[0]["out"].reshape(1, SEQ, D)
```

```python
from contextlib import ExitStack

import numpy as np

import concourse.bass as bass
from concourse import mybir

P = 128
D = 2048
SEQ = 256
T = SEQ // P
KT = D // P
F = 5632
W = 512
NF = F // W
ND = D // W
D_IN = 5376
WI = 448
NI = D_IN // WI
CH = 64
HD = 64
KV = 2
QUAD = 4
NQ = 16 // QUAD
RH = 4
RD = 256
A_K, A_V, R_Q, R_V, R_G = 1024, 1152, 1280, 3328, 4352
EPS = 1e-6

RAW = 4
LEAD = 4
HALF = 2 * W

G_FFN = [0, 3 * NF + NI + 4]
G_IN = 3 * NF
G_OUT = G_IN + NI
HALVES = 8 * (G_FFN[1] + 3 * NF)
X_FFN = [2, 2 + 4 * NF + 8]
X_OUT = 2 + 4 * NF

FFN1, MIX, FFN2, FINAL = range(4)

ALU = mybir.AluOpType
ACT = mybir.ActivationFunctionType
AX = mybir.AxisListType
F32 = mybir.dt.float32
F32R = mybir.dt.float32r
BF16 = mybir.dt.bfloat16


def build(nc, x_d, norms_d, g1, u1, d1, w_in, sinks_d, gn_d, w_out, g2, u2, d2, fw_d, ident_d, cos_d, sin_d,
          decay_d, out_d):
    ffn_w = [(g1, u1, d1), (g2, u2, d2)]
    with ExitStack() as ctx:
        def sb(name, shape, dt=F32, stack=ctx):
            return stack.enter_context(nc.sbuf_tensor(name, shape, dt))

        def sem(name):
            return ctx.enter_context(nc.semaphore(name))

        x = sb("x", [P, T, D])
        xT_hi = sb("xT_hi", [P, KT, SEQ], F32R)
        xT_lo = sb("xT_lo", [P, KT, SEQ], F32R)
        raw = sb("raw", [P, RAW, 4 * W])
        w_hi = sb("w_hi", [P, LEAD, 2, W], F32R)
        w_lo = sb("w_lo", [P, LEAD, 2, W], F32R)
        proj = sb("proj", [P, T, D_IN])
        attT_hi = sb("attT_hi", [P, KT // 2, SEQ], F32R)
        attT_lo = sb("attT_lo", [P, KT // 2, SEQ], F32R)
        ident = sb("ident", [P, P])
        norms = sb("norms", [P, 3, KT])
        gn_w = sb("gn_w", [P, 8])
        sinks = sb("sinks", [P, NQ * T * QUAD])
        neg_sinks = sb("neg_sinks", [P, NQ * T * QUAD])
        cos = sb("cos", [P, T, RD // 2])
        sin = sb("sin", [P, T, RD // 2])
        decay = sb("decay", [P, RH, 3 * P])
        junk = sb("junk", [P, T, W], BF16)
        sq = sb("sq", [P, 4, T, ND])
        ms = sb("ms", [P, 4, T])
        ms_eps = sb("ms_eps", [P, 4, T])
        rstd = sb("rstd", [P, 4, T])
        minus_half = sb("minus_half", [P, T])
        with ExitStack() as ffn:
            sg = sb("sg", [P, T, W], F32, ffn)
            h = sb("h", [P, T, W], F32, ffn)
            hT_hi = sb("hT_hi", [P, 4, SEQ], F32R, ffn)
            hT_lo = sb("hT_lo", [P, 4, SEQ], F32R, ffn)
        q_in = sb("q_in", [P, T, QUAD * HD])
        qT_full = sb("qT", [P, T, QUAD * P])
        qT = qT_full[0:HD, :, :]
        kT_all = sb("kT_all", [HD, KV, T, 2, P])
        v_all = sb("v_all", [P, KV, T, 2, HD])
        kT = sb("kT", [HD, T, 2, P])
        v = sb("v", [P, T, 2, HD])
        probs = sb("probs", [P, T, QUAD, P])
        probsT = sb("probsT", [P, T, QUAD * P])
        att = sb("att", [P, T, QUAD * HD])
        lmax = sb("lmax", [P, T * QUAD])
        neg_m = sb("neg_m", [P, T * QUAD])
        sink_m = sb("sink_m", [P, T * QUAD])
        sink_e = sb("sink_e", [P, T * QUAD])
        den = sb("den", [P, T * QUAD])
        den2 = sb("den2", [P, T * QUAD])
        rden = sb("rden", [P, T * QUAD])
        last_hT_hi, last_hT_lo = attT_hi[:, 0:4, :], attT_lo[:, 0:4, :]
        rot_a = q_in[:].rearrange("p t (q c) -> p t q c", q=2)
        rot_b = qT_full[:, 0, :].rearrange("p (t q c) -> p t q c", t=T, q=2)
        rqT = probs[:].rearrange("p t h c -> p (t h c)")[:, 0:2 * SEQ].rearrange("p (k s) -> p k s", k=2)
        rkT = probs[:].rearrange("p t h c -> p (t h c)")[:, 2 * SEQ:4 * SEQ].rearrange("p (k s) -> p k s", k=2)
        scores = probsT[:, 0, 0:3 * P]
        y_raw = probsT[:, 1, :].rearrange("p (t c) -> p t c", t=T)
        y = att
        final_w = proj[:, 0, 0:D]
        normed = proj[:, :, D:2 * D]
        stats = sb("stats", [P, RH, T, 6])
        mv = sb("mv", [P, RH, T, 2])
        var_eps = sb("var_eps", [P, RH, T])
        gn_rstd = sb("gn_rstd", [P, RH, T])
        ps = ctx.enter_context(nc.psum_tensor("ps", [P, 8, W], F32))
        B_GATE, B_UP, B_DOWN = 0, 2, 4

        raw_loaded = [sem(f"raw_loaded{s}") for s in range(RAW)]
        x_loaded = [sem(f"x_loaded{n}") for n in range(ND)]
        consts_loaded = sem("consts_loaded")
        mix_consts = sem("mix_consts")
        fw_loaded = sem("fw_loaded")
        hi_ready = sem("hi_ready")
        lo_ready = sem("lo_ready")
        half_used = sem("half_used")
        xT_turned = sem("xT_turned")
        xT_hi_ready = sem("xT_hi_ready")
        xT_lo_ready = sem("xT_lo_ready")
        sq_ready = sem("sq_ready")
        ms_added = sem("ms_added")
        ms_ready = sem("ms_ready")
        rstd_ready = sem("rstd_ready")
        half_const = sem("half_const")
        silu_done = sem("silu_done")
        h_ready = sem("h_ready")
        hT_turned = sem("hT_turned")
        hT_hi_ready = sem("hT_hi_ready")
        hT_lo_ready = sem("hT_lo_ready")
        x_added = sem("x_added")
        proj_ready = sem("proj_ready")
        neg_sinks_ready = sem("neg_sinks_ready")
        k_turned = sem("k_turned")
        kT_ready = sem("kT_ready")
        kT_zeroed = sem("kT_zeroed")
        v_ready = sem("v_ready")
        q_in_ready = sem("q_in_ready")
        kT_in_ready = sem("kT_in_ready")
        v_in_ready = sem("v_in_ready")
        q_turned = sem("q_turned")
        qT_ready = sem("qT_ready")
        logits_ready = sem("logits_ready")
        soft = sem("soft")
        neg_m_ready = sem("neg_m_ready")
        sink_m_ready = sem("sink_m_ready")
        probs_ready = sem("probs_ready")
        sink_e_ready = sem("sink_e_ready")
        probs_turned = sem("probs_turned")
        probsT_a = sem("probsT_a")
        probsT_b = sem("probsT_b")
        pv_done = sem("pv_done")
        att_ready = sem("att_ready")
        att_turned = sem("att_turned")
        attT_hi_ready = sem("attT_hi_ready")
        attT_lo_ready = sem("attT_lo_ready")
        rot = sem("rot")
        gate_ready = sem("gate_ready")
        rqk_turned = sem("rqk_turned")
        rqT_ready = sem("rqT_ready")
        rkT_ready = sem("rkT_ready")
        scores_done = sem("scores_done")
        scores_ready = sem("scores_ready")
        ret_done = sem("ret_done")
        stats_done = sem("stats_done")
        mv_ready = sem("mv_ready")
        var_eps_ready = sem("var_eps_ready")
        gn_ready = sem("gn_ready")
        y_raw_ready = sem("y_raw_ready")
        y_ready = sem("y_ready")
        y_turned = sem("y_turned")
        retT_hi_ready = sem("retT_hi_ready")
        retT_lo_ready = sem("retT_lo_ready")
        last_done = sem("last_done")
        x_final = sem("x_final")
        x_weighted = sem("x_weighted")
        out_ready = [sem(f"out_ready{t}") for t in range(T)]
        stored = sem("stored")

        block = ctx.enter_context(nc.Block())

        def f32(ap):
            return ap.bitcast(F32)

        def rot_view(half, head):
            qk = proj[:, :, R_Q:R_V].rearrange("p t (q h d) -> p t q h d", q=2, h=RH)
            return qk[:, :, :, head, half * (RD // 2):(half + 1) * (RD // 2)]

        @block.sync
        def _(sp):
            def load(g, s, src, width=W):
                if not (isinstance(g, int) and g == 0):
                    sp.wait_ge(lo_ready, 8 * g + 2 * s - 6)
                dst = raw[:, s, :].rearrange("p (k c) -> p k c", k=4)[:, :, 0:width]
                sp.dma_start(dst, src).then_inc(raw_loaded[s], 16)

            def rows(w, r0, c0, width=W):
                return w[bass.ds(r0, 4 * P), bass.ds(c0, width)].rearrange("(k p) c -> p k c", p=P)

            def load_ffn_in(f, g, i, loaded=0):
                for part in range(2):
                    for s in range(4):
                        if 4 * part + s >= loaded:
                            load(g + part, s, rows(ffn_w[f][part], 4 * P * s, i * W))

            def load_ffn_down(f, g, i):
                for s in range(4):
                    load(g, s, rows(ffn_w[f][2], i * W, s * W))

            def load_ffn(f):
                load_ffn_in(f, G_FFN[f], 0, 2 * (f == 0))
                if f == 0:
                    for t, t_d in ((sinks, sinks_d), (gn_w, gn_d), (cos, cos_d), (sin, sin_d), (decay, decay_d)):
                        sp.dma_start(t[:], t_d).then_inc(mix_consts, 16)
                else:
                    sp.wait_ge(retT_lo_ready, RH)
                    sp.dma_start(final_w, fw_d.partition_broadcast(P)).then_inc(fw_loaded, 16)
                with sp.Fori(1, NF) as i:
                    g = 3 * i + (G_FFN[f] - 1)
                    load_ffn_in(f, g, i)
                    load_ffn_down(f, g + 2, i - 1)
                load_ffn_down(f, G_FFN[f] + 3 * NF - 1, NF - 1)

            xv = x_d.rearrange("(t p) c -> p t c", p=P)
            sp.dma_start(ident[:], ident_d).then_inc(consts_loaded, 16)
            sp.dma_start(norms[:], norms_d).then_inc(consts_loaded, 16)
            for n in range(ND):
                sp.dma_start(x[:, :, n * W:(n + 1) * W], xv[:, :, n * W:(n + 1) * W]).then_inc(x_loaded[n], 16)
                if n < 2:
                    load(0, n, rows(g1, 4 * P * n, 0))
            load_ffn(0)
            with sp.Fori(0, NI) as b:
                for s in range(4):
                    load(b + G_IN, s, rows(w_in, 4 * P * s, b * WI, WI), WI)
            for part in range(2):
                for n in range(ND):
                    for u in range(2):
                        s = 2 * (n % 2) + u
                        load(G_OUT + 2 * part + n // 2, s, rows(w_out, D // 2 * part + 4 * P * u, n * W))
            load_ffn(1)
            ov = out_d.rearrange("(t p) c -> p t c", p=P)
            for t in range(T):
                for n in range(ND):
                    sp.wait_ge(out_ready[t], n + 1)
                    sp.dma_start(ov[:, t, n * W:(n + 1) * W], normed[:, t, n * W:(n + 1) * W]).then_inc(stored, 16)
            sp.wait_ge(stored, 16 * T * ND)

        @block.tensor
        def _(pe):
            def half(g, k, a_hi, a_lo, kt, bank, first, last, width=W):
                pe.wait_ge(lo_ready, 8 * g + (k + 1))
                for j in range(2):
                    for t in range(T):
                        out = ps[:, bank + t, 0:width]
                        xh, xl = (a[:, kt + j, t * P:(t + 1) * P] for a in (a_hi, a_lo))
                        wh, wl = (w[:, k % LEAD, j, 0:width] for w in (w_hi, w_lo))
                        pe.matmul(out, xh, wh, start=first and j == 0, stop=False)
                        pe.matmul(out, xh, wl, start=False, stop=False)
                        mm = pe.matmul(out, xl, wh, start=False, stop=last and j == 1)
                mm.then_inc(half_used, 1)

            def turn(bank, col, src):
                return pe.transpose(ps[0:src.shape[1], bank, col:col + P], src, ident[:])

            def turn_x(norm, n):
                if norm == FFN1:
                    pe.wait_ge(x_loaded[n], 16)
                else:
                    pe.wait_ge(x_added, {MIX: X_FFN[0] + 4 * (NF - 1), FFN2: X_OUT + 4}[norm] + n + 1)
                bank = (B_GATE, B_UP, B_DOWN, B_UP)[n]
                if n == 3:
                    pe.wait_ge(xT_lo_ready, 4 * norm + 2)
                elif n == 0 and norm == MIX:
                    pe.wait_ge(silu_done, T * NF)
                elif n == 1 and norm == MIX:
                    pe.wait_ge(h_ready, T * NF)
                elif n == 0 and norm == FFN2:
                    pe.wait_ge(rkT_ready, RH)
                    pe.wait_ge(rqT_ready, RH)
                elif n == 1 and norm == FFN2:
                    pe.wait_ge(retT_lo_ready, RH)
                    pe.wait_ge(y_raw_ready, T * RH)
                for j in range(4):
                    for t in range(T):
                        kt = 4 * n + j
                        mm = turn(bank + j // 2, (j % 2) * SEQ + t * P, x[:, t, kt * P:(kt + 1) * P])
                mm.then_inc(xT_turned, 1)

            def wide(norm, g, bank, width=W, h_of=None):
                for k in range(8):
                    if norm is not None and k % 2 == 0:
                        pe.wait_ge(xT_lo_ready, 4 * norm + k // 2 + 1)
                    half(g, k, xT_hi, xT_lo, 2 * k, bank, k == 0, k == 7, width)
                    if norm is not None and bank == B_GATE and k in (1, 3):
                        turn_x(norm, (k + 3) // 2)
                    if h_of is not None and k == 1:
                        turn_h(*h_of)

            def turn_h(f, i, bank=B_DOWN):
                c = 11 * f + i
                pe.wait_ge(h_ready, 2 * c + 2)
                if bank == B_DOWN:
                    pe.wait_ge(x_added, 4 * i + (X_FFN[f] - 1))
                for b in range(2):
                    for j in range(2):
                        for t in range(T):
                            mm = turn(bank + b, j * SEQ + t * P, h[:, t, (2 * b + j) * P:(2 * b + j + 1) * P])
                    mm.then_inc(hT_turned, 1)

            def down(f, g, i, last=False):
                pe.wait_ge(hT_lo_ready, 2 * (11 * f + i) + 2)
                for n in range(ND):
                    if n > 0:
                        pe.wait_ge(x_added, 4 * i + (X_FFN[f] + n - 1))
                    for u in range(2):
                        half(g, 2 * n + u, hT_hi, hT_lo, 2 * u, B_DOWN + 2 * (n % 2), u == 0, u == 1)
                    if last and n == 1:
                        turn_h(f, NF - 1, B_GATE)

            def last_down(f, g):
                i = NF - 1
                pe.wait_ge(hT_lo_ready, 2 * (11 * f + i) + 2)
                for n in range(ND):
                    pe.wait_ge(x_added, 4 * i + (X_FFN[f] + n - 1))
                    bank = B_DOWN + 2 * (n % 2)
                    if f == 1 and n == ND - 1:
                        pe.wait_ge(lo_ready, HALVES)
                        for t in range(T):
                            for kt in range(4):
                                wh, wl = (w[:, (6 + kt // 2) % LEAD, kt % 2, :] for w in (w_hi, w_lo))
                                xh, xl = (a[:, kt, t * P:(t + 1) * P] for a in (last_hT_hi, last_hT_lo))
                                pe.matmul(ps[:, bank + t, :], xh, wh, start=kt == 0, stop=False)
                                pe.matmul(ps[:, bank + t, :], xh, wl, start=False, stop=False)
                                mm = pe.matmul(ps[:, bank + t, :], xl, wh, start=False, stop=kt == 3)
                            mm.then_inc(last_done, 1)
                        break
                    for u in range(2):
                        half(g, 2 * n + u, last_hT_hi, last_hT_lo, 2 * u, bank, u == 0, u == 1)
                    if f == 0 and n in (1, 2):
                        turn_x(MIX, n - 1)
                if f == 0:
                    turn_x(MIX, 2)
                    turn_x(MIX, 3)

            def ffn(f):
                norm = (FFN1, FFN2)[f]
                wide(norm, G_FFN[f], B_GATE)
                wide(norm, G_FFN[f] + 1, B_UP)

                def step(i, last=False):
                    g = 3 * i + (G_FFN[f] - 1)
                    pe.wait_ge(silu_done, 2 * i + 22 * f)
                    wide(None, g, B_GATE, h_of=(f, i - 1))
                    pe.wait_ge(h_ready, 2 * i + 22 * f)
                    wide(None, g + 1, B_UP)
                    down(f, g + 2, i - 1, last)

                with pe.Fori(1, NF - 1) as i:
                    step(i)
                step(NF - 1, last=True)
                last_down(f, G_FFN[f] + 3 * NF - 1)

            def logits(quad):
                pe.wait_ge(kT_ready, 3)
                pe.wait_ge(qT_ready, quad)
                pe.wait_ge(kT_in_ready, quad)
                for t in range(T):
                    for hh in range(QUAD):
                        for c in range(2):
                            n = CH if t == 0 and c == 0 else 2 * CH
                            mm = pe.matmul(ps[c * CH:(c + 1) * CH, B_DOWN + 2 + t, hh * P:hh * P + n],
                                           qT[:, t, hh * P + c * CH:hh * P + (c + 1) * CH],
                                           kT[:, t, c, 0:n], start=True, stop=True)
                mm.then_inc(logits_ready, 1)

            def weigh(quad):
                pe.wait_ge(probsT_a, quad)
                pe.wait_ge(probsT_b, quad)
                pe.wait_ge(v_in_ready, quad)
                for t in range(T):
                    for hh in range(QUAD):
                        for c in range(2):
                            col = (t * QUAD + hh) * HD
                            mm = pe.matmul(ps[c * CH:(c + 1) * CH, B_DOWN + 2, col:col + HD],
                                           probsT[:, t, hh * P + c * CH:hh * P + (c + 1) * CH],
                                           v[:, t, c, :], start=True, stop=True)
                mm.then_inc(pv_done, 1)

            def in_projection():
                def pair(i, quad=None):
                    for e in range(2):
                        pe.wait_ge(proj_ready, 2 * i + (e + 1))
                        for k in range(8):
                            if quad is None and k % 2 == 0:
                                pe.wait_ge(xT_lo_ready, 4 * MIX + k // 2 + 1)
                            if quad is not None and (e, k) == (0, 3):
                                pe.wait_ge(attT_lo_ready, quad)
                            half(2 * i + (G_IN + e), k, xT_hi, xT_lo, 2 * k, B_GATE + 2 * e, k == 0, k == 7, WI)
                            if quad is not None and (e, k) == (0, 1):
                                pe.wait_ge(kT_ready, 3)
                                pe.wait_ge(q_in_ready, quad)
                                for t in range(T):
                                    for hh in range(QUAD):
                                        mm = turn(B_DOWN + t, hh * P, q_in[:, t, hh * HD:(hh + 1) * HD])
                                mm.then_inc(q_turned, 1)
                            if quad is not None and (e, k) == (0, 3):
                                logits(quad)
                            if quad is not None and (e, k) == (1, 0):
                                pe.wait_ge(probs_ready, quad)
                                for t in range(T):
                                    for hh in range(QUAD):
                                        mm = turn(B_DOWN + t, hh * P, probs[:, t, hh, :])
                                mm.then_inc(probs_turned, 1)
                            if quad is not None and (e, k) == (1, 2):
                                weigh(quad)
                            if quad is not None and (e, k) == (1, 5):
                                pe.wait_ge(att_ready, quad)
                                for k2 in range(2):
                                    for t in range(T):
                                        mm = turn(B_DOWN + 3, k2 * SEQ + t * P, att[:, t, k2 * P:(k2 + 1) * P])
                                mm.then_inc(att_turned, 1)

                with pe.Fori(0, 2) as i:
                    pair(i)
                pe.wait_ge(proj_ready, 2 + 3)
                for g in range(KV):
                    for t in range(T):
                        mm = turn(B_DOWN, (g * T + t) * P, proj[:, t, A_K + g * HD:A_K + (g + 1) * HD])
                mm.then_inc(k_turned, 1)
                with pe.Fori(1, NQ + 1) as quad:
                    pair(quad + 1, quad)

            def retention_start(hd):
                pe.wait_ge(rot, 6 * (hd + 1))
                pe.wait_ge(proj_ready, 2 + NI)
                if hd:
                    pe.wait_ge(rqT_ready, hd)
                    pe.wait_ge(rkT_ready, hd)
                for qk in range(2):
                    for dt in range(2):
                        for t in range(T):
                            c0 = R_Q + qk * RH * RD + hd * RD + dt * P
                            mm = turn(B_GATE + qk, dt * SEQ + t * P, proj[:, t, c0:c0 + P])
                mm.then_inc(rqk_turned, 1)

            def retention_scores(hd):
                pe.wait_ge(rqT_ready, hd + 1)
                pe.wait_ge(rkT_ready, hd + 1)
                if hd:
                    pe.wait_ge(retT_lo_ready, hd)
                for m in range(T):
                    for dt in range(2):
                        mm = pe.matmul(ps[:, B_UP, 2 * P * m:2 * P * m + SEQ - m * P], rkT[:, dt, m * P:(m + 1) * P],
                                       rqT[:, dt, m * P:SEQ], start=dt == 0, stop=dt == 1)
                mm.then_inc(scores_done, 1)

            def retention_out(hd):
                pe.wait_ge(scores_ready, hd + 1)
                if hd:
                    pe.wait_ge(y_raw_ready, T * hd)
                for t in range(T):
                    for m in range(t + 1):
                        c0 = 2 * P * m + (t - m) * P
                        mm = pe.matmul(ps[:, B_UP + 1, t * RD:(t + 1) * RD], scores[:, c0:c0 + P],
                                       proj[:, m, R_V + hd * RD:R_V + (hd + 1) * RD], start=m == 0, stop=m == t)
                mm.then_inc(ret_done, 1)

            def retention_turn(hd):
                pe.wait_ge(y_ready, hd + 1)
                for k2 in range(2):
                    for t in range(T):
                        mm = turn(B_UP, k2 * SEQ + t * P, y[:, t, k2 * P:(k2 + 1) * P])
                mm.then_inc(y_turned, 1)

            pe.wait_ge(consts_loaded, 32)
            turn_x(FFN1, 0)
            turn_x(FFN1, 1)
            ffn(0)
            in_projection()
            for q in range(32):
                n, k = q // 4 % ND, q % 4
                if q < 16:
                    if n == 0:
                        pe.wait_ge(attT_lo_ready, 1 + k + 1)
                    if n >= 2 and k == 0:
                        pe.wait_ge(x_added, X_OUT + n - 1)
                    half(G_OUT, q, attT_hi, attT_lo, 2 * k, B_DOWN + 2 * (n % 2), k == 0, k == 3)
                else:
                    if n == 0:
                        pe.wait_ge(retT_lo_ready, k + 1)
                    if k == 0:
                        pe.wait_ge(x_added, X_OUT + 4 + n - 1)
                    half(G_OUT, q, xT_hi, xT_lo, 8 + 2 * k, B_DOWN + 2 * (n % 2), k == 0, k == 3)
                if q < 16:
                    if k == 0:
                        retention_start(n)
                    if k == 2:
                        retention_scores(n)
                    if k == 3:
                        retention_out(n)
                if q % 4 == 1 and 5 <= q <= 17:
                    retention_turn(q // 4 - 1)
                if q in (22, 26):
                    turn_x(FFN2, (q - 22) // 4)
            ffn(1)

        @block.scalar
        def _(act):
            def split(g, k, first=False):
                g, k = g + k // 8, k % 8
                s = k // 2
                if not first:
                    act.wait_ge(half_used, 8 * g + (k + 1 - LEAD))
                if k % 2 == 0:
                    act.wait_ge(raw_loaded[s], 16 * g + 16)
                dst = w_hi[:, k % LEAD, :, :].rearrange("p k c -> p (k c)")
                act.activation(dst, raw[:, s, (k % 2) * HALF:(k % 2 + 1) * HALF], ACT.Copy).then_inc(hi_ready, 1)

            def position(g, k):
                if not (isinstance(g, int) and 8 * g + k + LEAD >= HALVES):
                    split(g, k + LEAD)

            def xT(norm, n):
                act.wait_ge(xT_turned, 4 * norm + n + 1)
                bank = (B_GATE, B_UP, B_DOWN, B_UP)[n]
                for j in range(4):
                    kt = 4 * n + j
                    a = act.activation(xT_hi[:, kt, :], ps[:, bank + j // 2, (j % 2) * SEQ:(j % 2 + 1) * SEQ],
                                       ACT.Copy, scale=norms[:, norm, kt:kt + 1])
                a.then_inc(xT_hi_ready, 1)

            def squares(norm, n, tiles=range(T)):
                if norm == FINAL and n == ND - 1:
                    act.wait_ge(x_final, tiles[0] + 1)
                elif norm == FFN1:
                    act.wait_ge(x_loaded[n], 16)
                else:
                    act.wait_ge(x_added, {MIX: X_FFN[0] + 4 * (NF - 1), FFN2: X_OUT + 4,
                                          FINAL: X_FFN[1] + 4 * (NF - 1)}[norm] + n + 1)
                for t in tiles:
                    c = T * (4 * norm + n) + t
                    if c >= T:
                        act.wait_ge(sq_ready, c - T + 1)
                    act.activation(junk[:, t, :], x[:, t, n * W:(n + 1) * W], ACT.Square,
                                   accum_out=sq[:, norm, t, n:n + 1]).then_inc(sq_ready, 1)

            def silu(f, g, i):
                act.wait_ge(half_used, 8 * g + 8)
                for t in range(T):
                    if not (isinstance(i, int) and f == 0):
                        act.wait_ge(h_ready, 2 * i + (22 * f + t - 1))
                    act.activation(sg[:, t, :], ps[:, B_GATE + t, :], ACT.Silu,
                                   scale=rstd[:, (FFN1, FFN2)[f], t:t + 1]).then_inc(silu_done, 1)

            def hT(f, i, dst=hT_hi, bank=B_DOWN):
                for b in range(2):
                    act.wait_ge(hT_turned, 2 * i + (22 * f + b + 1))
                    act.activation(dst[:, 2 * b:2 * b + 2, :].rearrange("p k s -> p (k s)"), ps[:, bank + b, :],
                                   ACT.Copy).then_inc(hT_hi_ready, 1)

            def ffn(f):
                g0 = G_FFN[f]
                for k in range(16):
                    position(g0, k)
                    if k in (1, 3):
                        xT((FFN1, FFN2)[f], (k + 3) // 2)
                    if k in (2, 3, 4, 5) and (f == 0 or k > 3):
                        squares((FFN1, FFN2)[f], k - 2)
                    if k == 7:
                        act.wait_ge(rstd_ready, (FFN1, FFN2)[f] + 1)
                        silu(f, g0, 0)

                def step(i, last=False):
                    g = 3 * i + (g0 - 1)
                    for k in range(24):
                        position(g, k)
                        if k == 1:
                            hT(f, i - 1)
                        if k == 7:
                            silu(f, g, i)
                        if last and k == 19:
                            hT(f, i, last_hT_hi, B_GATE)

                with act.Fori(1, NF - 1) as i:
                    step(i)
                step(NF - 1, last=True)
                g = g0 + 3 * NF - 1
                for k in range(8):
                    position(g, k)
                    if f == 0:
                        if k in (3, 5):
                            xT(MIX, (k - 3) // 2)
                            squares(MIX, (k - 3) // 2)
                        if k == 7:
                            for n in (2, 3):
                                xT(MIX, n)
                            for n in (2, 3):
                                squares(MIX, n)
                    elif k in (1, 3, 5):
                        squares(FINAL, k // 2)

            def proj_out(b, bank):
                act.wait_ge(half_used, 8 * b + (8 * G_IN + 8))
                for t in range(T):
                    a = act.activation(proj[:, t, bass.ds(b * WI, WI)], ps[:, bank + t, 0:WI], ACT.Copy,
                                       scale=rstd[:, MIX, t:t + 1])
                a.then_inc(proj_ready, 1)

            def in_pair(i, j=None):
                for k in range(16):
                    position(2 * i + G_IN, k)
                    if k == 7:
                        proj_out(2 * i, B_GATE)
                    if k == 15:
                        proj_out(2 * i + 1, B_UP)
                    if j is None:
                        continue
                    if k == 1:
                        act.wait_ge(q_turned, j + 1)
                        act.activation(qT.rearrange("p t c -> p (t c)"),
                                       ps[0:HD, B_DOWN:B_DOWN + 2, :].rearrange("p t c -> p (t c)"),
                                       ACT.Copy).then_inc(qT_ready, 1)
                    if k == 4:
                        act.wait_ge(neg_m_ready, j + 1)
                        for t in range(T):
                            for hh in range(QUAD):
                                c = t * QUAD + hh
                                a = act.activation(probs[:, t, hh, :], ps[:, B_DOWN + 2 + t, hh * P:(hh + 1) * P],
                                                   ACT.Exp, bias=neg_m[:, c:c + 1], scale=HD ** -0.5,
                                                   accum_out=den[:, c:c + 1])
                        a.then_inc(probs_ready, 1)
                        act.wait_ge(sink_m_ready, j + 1)
                        act.activation(sink_e[:], sink_m[:], ACT.Exp).then_inc(sink_e_ready, 1)
                    if k == 8:
                        act.wait_ge(probs_turned, j + 1)
                        act.activation(probsT[:, 0, :], ps[:, B_DOWN, :], ACT.Copy).then_inc(probsT_a, 1)
                    if k == 13:
                        act.wait_ge(att_turned, j + 1)
                        act.activation(attT_hi[:, bass.ds(2 * j, 2), :], ps[:, B_DOWN + 3, :].rearrange(
                            "p (k s) -> p k s", k=2), ACT.Copy).then_inc(attT_hi_ready, 1)

            act.wait_ge(consts_loaded, 32)
            act.sem_inc(proj_ready, 2)
            for n in range(2):
                xT(FFN1, n)
                split(0, 2 * n, first=True)
                split(0, 2 * n + 1, first=True)
            ffn(0)
            act.wait_ge(rstd_ready, MIX + 1)
            with act.Fori(0, 2) as i:
                in_pair(i)
            with act.Fori(0, NQ) as j:
                in_pair(j + 2, j)
            for q in range(32):
                position(G_OUT, q)
                if q % 4 == 0 and q < 16:
                    hd = q // 4
                    act.wait_ge(rqk_turned, hd + 1)
                    act.activation(rqT.rearrange("p k s -> p (k s)"), ps[:, B_GATE, :],
                                   ACT.Copy).then_inc(rqT_ready, 1)
                    gate = proj[:, :, R_G + hd * RD:R_G + (hd + 1) * RD]
                    if hd == 0:
                        act.wait_ge(proj_ready, 2 + NI)
                    act.activation(gate, gate, ACT.Silu).then_inc(gate_ready, 1)
                if q % 4 == 0 and 4 <= q <= 16:
                    hd = q // 4 - 1
                    act.wait_ge(gn_ready, hd + 1)
                    act.wait_ge(y_raw_ready, T * (hd + 1))
                    if hd:
                        act.wait_ge(y_turned, hd)
                    for t in range(T):
                        a = act.activation(y[:, t, :], y_raw[:, t, :], ACT.Copy, scale=gn_rstd[:, hd, t:t + 1])
                    a.then_inc(y_ready, 1)
                if q % 4 == 1 and 5 <= q <= 17:
                    hd = q // 4 - 1
                    act.wait_ge(y_turned, hd + 1)
                    for k2 in range(2):
                        a = act.activation(xT_hi[:, 8 + 2 * hd + k2, :], ps[:, B_UP, k2 * SEQ:(k2 + 1) * SEQ],
                                           ACT.Copy, scale=gn_w[:, 2 * hd + k2:2 * hd + k2 + 1])
                    a.then_inc(retT_hi_ready, 1)
                if q in (22, 26):
                    xT(FFN2, (q - 22) // 4)
                    squares(FFN2, (q - 22) // 4)
            ffn(1)

            def scale_first(n):
                yb = normed[:, 0, n * W:(n + 1) * W]
                act.activation(yb, yb, ACT.Copy, scale=rstd[:, FINAL, 0:1]).then_inc(out_ready[0], 1)

            squares(FINAL, ND - 1, (0,))
            act.wait_ge(rstd_ready, FINAL + 1)
            act.wait_ge(x_weighted, 2 * (ND - 1) + 1)
            scale_first(0)
            squares(FINAL, ND - 1, (1,))
            for n in range(1, ND):
                scale_first(n)

        @block.vector
        def _(dve):
            def split(g, k):
                g, k = g + k // 8, k % 8
                dve.wait_ge(hi_ready, 8 * g + (k + 1))
                flat = "p k c -> p (k c)"
                dve.tensor_tensor(w_lo[:, k % LEAD, :, :].rearrange(flat),
                                  raw[:, k // 2, (k % 2) * HALF:(k % 2 + 1) * HALF],
                                  f32(w_hi[:, k % LEAD, :, :].rearrange(flat)), ALU.subtract).then_inc(lo_ready, 1)

            def position(g, k):
                if not (isinstance(g, int) and 8 * g + k + LEAD >= HALVES):
                    split(g, k + LEAD)

            def xT(norm, n):
                dve.wait_ge(xT_hi_ready, 4 * norm + n + 1)
                bank = (B_GATE, B_UP, B_DOWN, B_UP)[n]
                for j in range(4):
                    kt = 4 * n + j
                    a = dve.scalar_tensor_tensor(out=xT_lo[:, kt, :],
                                                 in0=ps[:, bank + j // 2, (j % 2) * SEQ:(j % 2 + 1) * SEQ],
                                                 scalar=norms[:, norm, kt:kt + 1], in1=f32(xT_hi[:, kt, :]),
                                                 op0=ALU.mult, op1=ALU.subtract)
                a.then_inc(xT_lo_ready, 1)

            def mean_square(norm, t0=0, t1=T):
                dve.wait_ge(sq_ready, T * (4 * norm + 3) + t1)
                dve.tensor_reduce(ms[:, norm, t0:t1], sq[:, norm, t0:t1, :], AX.X, ALU.add).then_inc(ms_added, 1)
                dve.wait_ge(ms_added, norm + t0 + 1)
                dve.tensor_scalar(ms_eps[:, norm, t0:t1], ms[:, norm, t0:t1], 1.0 / D, EPS, ALU.mult,
                                  ALU.add).then_inc(ms_ready, 1)

            def gated(f, g, i):
                dve.wait_ge(half_used, 8 * g + 16)
                for t in range(T):
                    dve.wait_ge(silu_done, 2 * i + (22 * f + t + 1))
                    if not (isinstance(i, int) and f == 0) and t == 0:
                        dve.wait_ge(hT_turned, 2 * i + 22 * f)
                    dve.scalar_tensor_tensor(out=h[:, t, :], in0=ps[:, B_UP + t, :],
                                             scalar=rstd[:, (FFN1, FFN2)[f], t:t + 1], in1=sg[:, t, :],
                                             op0=ALU.mult, op1=ALU.mult).then_inc(h_ready, 1)

            def hT(f, i, hi=hT_hi, lo=hT_lo, bank=B_DOWN):
                for b in range(2):
                    dve.wait_ge(hT_hi_ready, 2 * i + (22 * f + b + 1))
                    dve.tensor_tensor(lo[:, 2 * b:2 * b + 2, :].rearrange("p k s -> p (k s)"), ps[:, bank + b, :],
                                      f32(hi[:, 2 * b:2 * b + 2, :].rearrange("p k s -> p (k s)")),
                                      ALU.subtract).then_inc(hT_lo_ready, 1)

            def add(g, k, n, scale):
                dve.wait_ge(half_used, 8 * g + (k + 1))
                for t in range(T):
                    xb = x[:, t, n * W:(n + 1) * W]
                    a = dve.scalar_tensor_tensor(out=xb, in0=ps[:, B_DOWN + 2 * (n % 2) + t, :], scalar=scale,
                                                 in1=xb, op0=ALU.mult, op1=ALU.add)
                a.then_inc(x_added, 1)

            def ffn(f):
                g0 = G_FFN[f]
                for k in range(16):
                    position(g0, k)
                    if k in (1, 3):
                        xT((FFN1, FFN2)[f], (k + 3) // 2)
                    if k == 5:
                        mean_square((FFN1, FFN2)[f])
                    if k == 15:
                        dve.wait_ge(rstd_ready, (FFN1, FFN2)[f] + 1)
                        gated(f, g0, 0)

                def step(i, last=False):
                    g = 3 * i + (g0 - 1)
                    for k in range(24):
                        position(g, k)
                        if k == 1:
                            hT(f, i - 1)
                        if k == 15:
                            gated(f, g, i)
                        if k >= 16 and k % 2:
                            add(g, k, (k - 16) // 2, 0.5)
                        if last and k == 19:
                            hT(f, i, last_hT_hi, last_hT_lo, B_GATE)

                with dve.Fori(1, NF - 1) as i:
                    step(i)
                step(NF - 1, last=True)
                g = g0 + 3 * NF - 1
                if f == 1:
                    dve.wait_ge(fw_loaded, 16)
                for k in range(8):
                    if k < 7:
                        position(g, k)
                    if k % 2 and (f == 0 or k < 7):
                        add(g, k, k // 2, 0.5)
                    if f == 1 and k in (1, 3, 5):
                        for t in range(T):
                            weigh_final(t, k // 2)
                    if f == 0 and k == 7:
                        position(g, k)
                    if f == 0 and k in (3, 5):
                        xT(MIX, (k - 3) // 2)
                    if f == 0 and k == 7:
                        xT(MIX, 2)
                        xT(MIX, 3)
                        mean_square(MIX)

            def weigh_final(t, n):
                cols = slice(n * W, (n + 1) * W)
                if t == 0 and n < ND - 1:
                    dve.wait_ge(x_added, X_FFN[1] + 4 * (NF - 1) + n + 1)
                dve.tensor_tensor(normed[:, t, cols], x[:, t, cols], final_w[:, cols],
                                  ALU.mult).then_inc(x_weighted, 1)

            def in_pair(i, j=None):
                for k in range(16):
                    position(2 * i + G_IN, k)
                    if j is None:
                        continue
                    if k == 3:
                        dve.wait_ge(logits_ready, j + 1)
                        first = ps[0:CH, B_DOWN + 2, :].rearrange("p (h c) -> p h c", h=QUAD)
                        dve.memset(first[:, :, CH:2 * CH], -3.0e38).then_inc(soft, 1)
                        dve.wait_ge(soft, 4 * j + 1)
                        dve.tensor_reduce(lmax[:], ps[:, B_DOWN + 2:B_DOWN + 4, :].rearrange(
                            "p t (h c) -> p (t h) c", h=QUAD), AX.X, ALU.max).then_inc(soft, 1)
                        dve.wait_ge(soft, 4 * j + 2)
                        dve.scalar_tensor_tensor(out=neg_m[:], in0=lmax[:], scalar=-HD ** -0.5,
                                                 in1=neg_sinks[:, bass.ds(8 * j, 8)], op0=ALU.mult,
                                                 op1=ALU.min).then_inc(neg_m_ready, 1)
                        dve.wait_ge(neg_m_ready, j + 1)
                        dve.tensor_tensor(sink_m[:], sinks[:, bass.ds(8 * j, 8)], neg_m[:],
                                          ALU.add).then_inc(sink_m_ready, 1)
                    if k == 8:
                        dve.wait_ge(sink_e_ready, j + 1)
                        dve.tensor_tensor(den2[:], den[:], sink_e[:], ALU.add).then_inc(soft, 1)
                        dve.wait_ge(soft, 4 * j + 3)
                        dve.reciprocal(rden[:], den2[:]).then_inc(soft, 1)
                        dve.wait_ge(probs_turned, j + 1)
                        dve.tensor_copy(probsT[:, 1, :], ps[:, B_DOWN + 1, :]).then_inc(probsT_b, 1)
                    if k == 10:
                        dve.wait_ge(pv_done, j + 1)
                        dve.wait_ge(soft, 4 * j + 4)
                        dve.tensor_tensor(att[:].rearrange("p t (h d) -> p (t h) d", h=QUAD),
                                          ps[:, B_DOWN + 2, :].rearrange("p (h d) -> p h d", d=HD),
                                          rden[:].unsqueeze(2).to_broadcast([P, T * QUAD, HD]),
                                          ALU.mult).then_inc(att_ready, 1)
                    if k == 13:
                        dve.wait_ge(attT_hi_ready, j + 1)
                        dve.tensor_tensor(attT_lo[:, bass.ds(2 * j, 2), :],
                                          ps[:, B_DOWN + 3, :].rearrange("p (k s) -> p k s", k=2),
                                          f32(attT_hi[:, bass.ds(2 * j, 2), :]),
                                          ALU.subtract).then_inc(attT_lo_ready, 1)

            dve.sem_inc(x_added, X_FFN[0])
            dve.sem_inc(attT_lo_ready, 1)
            dve.wait_ge(consts_loaded, 32)
            for n in range(2):
                xT(FFN1, n)
                split(0, 2 * n)
                split(0, 2 * n + 1)
            ffn(0)
            dve.wait_ge(mix_consts, 16 * 5)
            dve.tensor_scalar(neg_sinks[:], sinks[:], -1.0, None, ALU.mult).then_inc(neg_sinks_ready, 1)
            with dve.Fori(0, 2) as i:
                in_pair(i)
            dve.wait_ge(k_turned, 1)
            dve.wait_ge(kT_zeroed, 1)
            turned = ps[0:HD, B_DOWN, :].rearrange("p (g t c) -> p g t c", g=KV, t=T)
            dve.tensor_copy(kT_all[:, :, :, 1, :], turned).then_inc(kT_ready, 1)
            dve.tensor_copy(kT_all[:, :, :, 0, 0:CH], turned[:, :, :, 0:CH]).then_inc(kT_ready, 1)
            dve.tensor_copy(kT_all[:, :, 1, 0, CH:2 * CH], turned[:, :, 0, CH:2 * CH]).then_inc(kT_ready, 1)
            dve.wait_ge(neg_sinks_ready, 1)
            with dve.Fori(0, NQ) as j:
                in_pair(j + 2, j)
            for q in range(32):
                position(G_OUT, q)
                if q % 4 == 3:
                    add(G_OUT, q, q // 4 % ND, 1.0)
                if q % 4 == 0 and q < 16:
                    hd = q // 4
                    dve.wait_ge(rqk_turned, hd + 1)
                    dve.tensor_copy(rkT.rearrange("p k s -> p (k s)"), ps[:, B_GATE + 1, :]).then_inc(rkT_ready, 1)
                if q % 4 == 2 and q < 16:
                    hd = q // 4
                    dve.wait_ge(scores_done, hd + 1)
                    dve.tensor_tensor(scores, ps[:, B_UP, 0:3 * P], decay[:, hd, :], ALU.mult).then_inc(scores_ready, 1)
                if q % 4 == 3 and q < 16:
                    hd = q // 4
                    dve.wait_ge(ret_done, hd + 1)
                    for t in range(T):
                        dve.bn_stats(stats[:, hd, t, :], ps[:, B_UP + 1, t * RD:(t + 1) * RD]).then_inc(stats_done, 1)
                    for t in range(T):
                        dve.wait_ge(stats_done, T * hd + t + 1)
                        dve.bn_aggr(mv[:, hd, t, :], stats[:, hd, t, :]).then_inc(mv_ready, 1)
                    dve.wait_ge(gate_ready, hd + 1)
                    dve.wait_ge(mv_ready, T * (hd + 1))
                    if hd:
                        dve.wait_ge(y_ready, hd)
                    for t in range(T):
                        dve.scalar_tensor_tensor(out=y_raw[:, t, :], in0=ps[:, B_UP + 1, t * RD:(t + 1) * RD],
                                                 scalar=mv[:, hd, t, 0:1],
                                                 in1=proj[:, t, R_G + hd * RD:R_G + (hd + 1) * RD],
                                                 op0=ALU.subtract, op1=ALU.mult).then_inc(y_raw_ready, 1)
                if q % 4 == 1 and 5 <= q <= 17:
                    hd = q // 4 - 1
                    dve.wait_ge(retT_hi_ready, hd + 1)
                    for k2 in range(2):
                        a = dve.scalar_tensor_tensor(
                            out=xT_lo[:, 8 + 2 * hd + k2, :], in0=ps[:, B_UP, k2 * SEQ:(k2 + 1) * SEQ],
                            scalar=gn_w[:, 2 * hd + k2:2 * hd + k2 + 1], in1=f32(xT_hi[:, 8 + 2 * hd + k2, :]),
                            op0=ALU.mult, op1=ALU.subtract)
                    a.then_inc(retT_lo_ready, 1)
                if q in (22, 26):
                    xT(FFN2, (q - 22) // 4)
            ffn(1)
            for t in range(T):
                dve.wait_ge(last_done, t + 1)
                xb = x[:, t, (ND - 1) * W:]
                dve.scalar_tensor_tensor(out=xb, in0=ps[:, B_DOWN + 2 + t, :], scalar=0.5, in1=xb, op0=ALU.mult,
                                         op1=ALU.add).then_inc(x_final, 1)
                dve.wait_ge(x_final, t + 1)
                weigh_final(t, ND - 1)
                mean_square(FINAL, t, t + 1)
            dve.wait_ge(rstd_ready, FINAL + T)
            dve.wait_ge(x_weighted, T * ND)
            for n in range(ND):
                yb = normed[:, 1, n * W:(n + 1) * W]
                dve.tensor_scalar(yb, yb, rstd[:, FINAL, 1:2], None, ALU.mult).then_inc(out_ready[1], 1)

        @block.gpsimd
        def _(pool):
            def rsqrt_of_norm(norm, t0=0, t1=T):
                pool.wait_ge(ms_ready, norm + t0 + 1)
                pool.tensor_tensor(rstd[:, norm, t0:t1], ms_eps[:, norm, t0:t1], minus_half[:, t0:t1],
                                   ALU.pow).then_inc(rstd_ready, 1)

            def stage(j):
                again = not isinstance(j, int)
                if again:
                    pool.wait_ge(q_turned, j)
                    pool.wait_ge(v_in_ready, j)
                pool.tensor_copy(q_in[:], proj[:, :, bass.ds(j * QUAD * HD, QUAD * HD)]).then_inc(q_in_ready, 1)
                if again:
                    pool.wait_ge(logits_ready, j)
                else:
                    pool.wait_ge(kT_ready, 3)
                pool.wait_ge(q_in_ready, j + 1)
                pool.tensor_copy(kT[:], kT_all[:, bass.ds(j // 2, 1), :, :, :].rearrange(
                    "p g t v c -> p (g t) v c")).then_inc(kT_in_ready, 1)
                if again:
                    pool.wait_ge(pv_done, j)
                pool.wait_ge(kT_in_ready, j + 1)
                pool.tensor_copy(v[:], v_all[:, bass.ds(j // 2, 1), :, :, :].rearrange(
                    "p g t v c -> p (g t) v c")).then_inc(v_in_ready, 1)

            def rotate(hd):
                t1, t2 = rot_view(0, hd), rot_view(1, hd)
                c, s = (a[:].unsqueeze(2).to_broadcast([P, T, 2, RD // 2]) for a in (cos, sin))
                step = 6 * hd
                if hd:
                    pool.wait_ge(rot, step)
                pool.tensor_tensor(rot_a, t1, s, ALU.mult).then_inc(rot, 1)
                pool.tensor_tensor(rot_b, t2, s, ALU.mult).then_inc(rot, 1)
                pool.wait_ge(rot, step + 2)
                pool.tensor_tensor(t1, t1, c, ALU.mult).then_inc(rot, 1)
                pool.tensor_tensor(t2, t2, c, ALU.mult).then_inc(rot, 1)
                pool.wait_ge(rot, step + 4)
                pool.tensor_tensor(t1, t1, rot_b, ALU.subtract).then_inc(rot, 1)
                pool.tensor_tensor(t2, t2, rot_a, ALU.add).then_inc(rot, 1)

            def rsqrt_of_head(hd):
                pool.wait_ge(mv_ready, T * (hd + 1))
                pool.tensor_scalar(var_eps[:, hd, :], mv[:, hd, :, 1], EPS, None, ALU.add).then_inc(var_eps_ready, 1)
                pool.wait_ge(var_eps_ready, hd + 1)
                pool.tensor_tensor(gn_rstd[:, hd, :], var_eps[:, hd, :], minus_half[:], ALU.pow).then_inc(gn_ready, 1)

            pool.memset(minus_half[:], -0.5).then_inc(half_const, 1)
            pool.wait_ge(half_const, 1)
            rsqrt_of_norm(FFN1)
            rsqrt_of_norm(MIX)
            pool.wait_ge(rstd_ready, MIX + 1)
            pool.memset(kT_all[:, :, 0, 0, CH:2 * CH], 0.0).then_inc(kT_zeroed, 1)
            pool.wait_ge(kT_zeroed, 1)
            pool.memset(v_all[CH:P, :, 0, 0, :], 0.0).then_inc(v_ready, 1)
            pool.wait_ge(proj_ready, 2 + 3)
            pool.wait_ge(v_ready, 1)
            vals = proj[:, :, A_V:R_Q].rearrange("p t (g d) -> p g t d", g=KV)
            pool.tensor_copy(v_all[:, :, :, 1, :], vals).then_inc(v_ready, 1)
            pool.wait_ge(v_ready, 2)
            pool.tensor_copy(v_all[0:CH, :, :, 0, :], vals[0:CH]).then_inc(v_ready, 1)
            pool.wait_ge(v_ready, 3)
            pool.tensor_copy(v_all[CH:P, :, 1, 0, :], vals[CH:P, :, 0, :]).then_inc(v_ready, 1)
            pool.wait_ge(v_ready, 4)
            stage(0)
            with pool.Fori(1, NQ) as j:
                stage(j)
            pool.wait_ge(v_in_ready, NQ)
            pool.wait_ge(proj_ready, 2 + 8)
            pool.wait_ge(mix_consts, 16 * 5)
            pool.wait_ge(logits_ready, NQ)
            for hd in range(RH):
                rotate(hd)
            for hd in range(RH):
                rsqrt_of_head(hd)
            rsqrt_of_norm(FFN2)
            for t in range(T):
                rsqrt_of_norm(FINAL, t, t + 1)


def constants():
    inv = np.float32(10000.0) ** (-np.arange(0, RD, 2, dtype=np.float32) / np.float32(RD))
    ang = np.arange(SEQ, dtype=np.float32)[:, None] * inv.astype(np.float32)[None, :]
    by_token = [f(ang).astype(np.float32).reshape(T, P, RD // 2).transpose(1, 0, 2) for f in (np.cos, np.sin)]
    log_gamma = np.log(1.0 - 2.0 ** (-5.0 - np.arange(RH, dtype=np.float64)))
    n = np.arange(SEQ)
    dist = n[None, :] - n[:, None]
    full = np.where(dist >= 0, np.exp(log_gamma[:, None, None] * np.maximum(dist, 0)), 0.0) * RD ** -0.5
    tiles = np.concatenate([full[:, 0:P, :], full[:, P:SEQ, P:SEQ]], axis=2)
    return {"ident": np.eye(P, dtype=np.float32), "cos": by_token[0], "sin": by_token[1],
            "decay": tiles.transpose(1, 0, 2).astype(np.float32)}


def kernel(**inputs):
    import concourse.bacc as bacc
    from concourse.bass_utils import run_bass_kernel_spmd

    a = {k: np.asarray(v) for k, v in inputs.items()}

    def by_feature(w, n):
        return w.reshape(n, P).T

    arrays = {
        "x": a["x"].reshape(SEQ, D),
        "norms": np.stack([by_feature(a[k], KT) for k in ("norm_ffn1_w", "norm_mix_w", "norm_ffn2_w")], axis=1),
        "g1": a["ffn1_w_gate"][0], "u1": a["ffn1_w_up"][0], "d1": a["ffn1_w_down"][0],
        "w_in": a["w_in"][0],
        "sinks": np.broadcast_to(a["attn_sinks"].reshape(1, NQ, 1, QUAD), (P, NQ, T, QUAD)).reshape(P, -1),
        "gn": by_feature(a["ret_gn_w"], 8),
        "w_out": a["w_out"][0],
        "g2": a["ffn2_w_gate"][0], "u2": a["ffn2_w_up"][0], "d2": a["ffn2_w_down"][0],
        "fw": a["norm_final_w"],
        **constants(),
    }
    nc = bacc.Bacc("TRN2", target_bir_lowering=False, num_devices=1)
    feed, args = {}, []
    for name, arr in arrays.items():
        arr = np.ascontiguousarray(arr)
        feed[f"in_{name}"] = arr
        args.append(nc.dram_tensor(f"in_{name}", arr.shape, mybir.dt.from_np(arr.dtype), kind="ExternalInput").ap())
    out = nc.dram_tensor("out", (SEQ, D), F32, kind="ExternalOutput").ap()
    build(nc, *args, out)
    r = run_bass_kernel_spmd(nc, [feed], core_ids=[0])
    return r.results[0]["out"].reshape(1, SEQ, D)
```

```python
from contextlib import ExitStack

import numpy as np

import concourse.bass as bass
from concourse import mybir

P = 128
D = 2048
SEQ = 256
T = SEQ // P
KT = D // P
F = 5632
W = 512
NF = F // W
ND = D // W
D_IN = 5376
WI = 448
NI = D_IN // WI
CH = 64
HD = 64
KV = 2
QUAD = 4
NQ = 16 // QUAD
RH = 4
RD = 256
A_K, A_V, R_Q, R_V, R_G = 1024, 1152, 1280, 3328, 4352
EPS = 1e-6

RAW = 4
LEAD = 4
HALF = 2 * W

G_FFN = [0, 3 * NF + NI + 4]
G_IN = 3 * NF
G_OUT = G_IN + NI
HALVES = 8 * (G_FFN[1] + 3 * NF)
X_FFN = [2, 2 + 4 * NF + 8]
X_OUT = 2 + 4 * NF

FFN1, MIX, FFN2, FINAL = range(4)
PAIRS = KT // 2
LATE = 2

X_PIECES = [(0, 2), (2, 4), (4, 8), (8, 12), (12, 16)]
X_PIECE_OF_PAIR = [next(i for i, (a, b) in enumerate(X_PIECES) if a <= 2 * p < b) for p in range(PAIRS)]

ALU = mybir.AluOpType
ACT = mybir.ActivationFunctionType
AX = mybir.AxisListType
F32 = mybir.dt.float32
F32R = mybir.dt.float32r
BF16 = mybir.dt.bfloat16


def build(nc, x_d, norms_d, g1, u1, d1, w_in, sinks_d, gn_d, w_out, g2, u2, d2, fw_d, ident_d, cos_d, sin_d,
          decay_d, out_d):
    ffn_w = [(g1, u1, d1), (g2, u2, d2)]
    with ExitStack() as ctx:
        def sb(name, shape, dt=F32, stack=ctx):
            return stack.enter_context(nc.sbuf_tensor(name, shape, dt))

        def sem(name):
            return ctx.enter_context(nc.semaphore(name))

        x = sb("x", [P, T, D])
        xT_hi = sb("xT_hi", [P, KT, SEQ], F32R)
        xT_lo = sb("xT_lo", [P, KT, SEQ], F32R)
        raw = sb("raw", [P, RAW, 4 * W])
        w_hi = sb("w_hi", [P, LEAD, 2, W], F32R)
        w_lo = sb("w_lo", [P, LEAD, 2, W], F32R)
        proj = sb("proj", [P, T, D_IN])
        attT_hi = sb("attT_hi", [P, KT // 2, SEQ], F32R)
        attT_lo = sb("attT_lo", [P, KT // 2, SEQ], F32R)
        ident = sb("ident", [P, P])
        norms = sb("norms", [P, 3, KT])
        gn_w = sb("gn_w", [P, 8])
        sinks = sb("sinks", [P, NQ * T * QUAD])
        neg_sinks = sb("neg_sinks", [P, NQ * T * QUAD])
        cos = sb("cos", [P, T, RD // 2])
        sin = sb("sin", [P, T, RD // 2])
        decay = sb("decay", [P, RH, 3 * P])
        junk = sb("junk", [P, T, W], BF16)
        sq = sb("sq", [P, 4, T, ND])
        ms = sb("ms", [P, 4, T])
        ms_eps = sb("ms_eps", [P, 4, T])
        rstd = sb("rstd", [P, 4, T])
        minus_half = sb("minus_half", [P, T])
        with ExitStack() as ffn:
            sg = sb("sg", [P, T, W], F32, ffn)
            h = sb("h", [P, T, W], F32, ffn)
            hT_hi = sb("hT_hi", [P, 4, SEQ], F32R, ffn)
            hT_lo = sb("hT_lo", [P, 4, SEQ], F32R, ffn)
        q_in = sb("q_in", [P, T, QUAD * HD])
        qT_full = sb("qT", [P, T, QUAD * P])
        qT = qT_full[0:HD, :, :]
        kT_all = sb("kT_all", [HD, KV, T, 2, P])
        v_all = sb("v_all", [P, KV, T, 2, HD])
        kT = sb("kT", [HD, T, 2, P])
        v = sb("v", [P, T, 2, HD])
        probs = sb("probs", [P, T, QUAD, P])
        probsT = sb("probsT", [P, T, QUAD * P])
        att = sb("att", [P, T, QUAD * HD])
        lmax = sb("lmax", [P, T * QUAD])
        neg_m = sb("neg_m", [P, T * QUAD])
        sink_m = sb("sink_m", [P, T * QUAD])
        sink_e = sb("sink_e", [P, T * QUAD])
        den = sb("den", [P, T * QUAD])
        den2 = sb("den2", [P, T * QUAD])
        rden = sb("rden", [P, T * QUAD])
        last_hT_hi, last_hT_lo = attT_hi[:, 0:4, :], attT_lo[:, 0:4, :]
        rot_a = q_in[:].rearrange("p t (q c) -> p t q c", q=2)
        rot_b = qT_full[:, 0, :].rearrange("p (t q c) -> p t q c", t=T, q=2)
        rqT = probs[:].rearrange("p t h c -> p (t h c)")[:, 0:2 * SEQ].rearrange("p (k s) -> p k s", k=2)
        rkT = probs[:].rearrange("p t h c -> p (t h c)")[:, 2 * SEQ:4 * SEQ].rearrange("p (k s) -> p k s", k=2)
        scores = probsT[:, 0, 0:3 * P]
        y_raw = probsT[:, 1, :].rearrange("p (t c) -> p t c", t=T)
        y = att
        final_w = proj[:, 0, 0:D]
        normed = proj[:, :, D:2 * D]
        stats = sb("stats", [P, RH, T, 6])
        mv = sb("mv", [P, RH, T, 2])
        var_eps = sb("var_eps", [P, RH, T])
        gn_rstd = sb("gn_rstd", [P, RH, T])
        ps = ctx.enter_context(nc.psum_tensor("ps", [P, 8, W], F32))
        B_GATE, B_UP, B_DOWN = 0, 2, 4

        raw_loaded = [sem(f"raw_loaded{s}") for s in range(RAW)]
        first_half_loaded = sem("first_half_loaded")
        zeros_ready = sem("zeros_ready")
        x_loaded = [sem(f"x_loaded{n}") for n in range(len(X_PIECES))]
        consts_loaded = sem("consts_loaded")
        mix_consts = sem("mix_consts")
        fw_loaded = sem("fw_loaded")
        hi_ready = sem("hi_ready")
        lo_ready = sem("lo_ready")
        half_used = sem("half_used")
        xT_turned = sem("xT_turned")
        xT_hi_ready = sem("xT_hi_ready")
        xT_lo_ready = sem("xT_lo_ready")
        sq_ready = sem("sq_ready")
        ms_added = sem("ms_added")
        ms_ready = sem("ms_ready")
        rstd_ready = sem("rstd_ready")
        half_const = sem("half_const")
        silu_done = sem("silu_done")
        h_ready = sem("h_ready")
        hT_turned = sem("hT_turned")
        hT_hi_ready = sem("hT_hi_ready")
        hT_lo_ready = sem("hT_lo_ready")
        x_added = sem("x_added")
        proj_ready = sem("proj_ready")
        neg_sinks_ready = sem("neg_sinks_ready")
        k_turned = sem("k_turned")
        kT_ready = sem("kT_ready")
        kT_zeroed = sem("kT_zeroed")
        v_ready = sem("v_ready")
        q_in_ready = sem("q_in_ready")
        kT_in_ready = sem("kT_in_ready")
        v_in_ready = sem("v_in_ready")
        q_turned = sem("q_turned")
        qT_ready = sem("qT_ready")
        logits_ready = sem("logits_ready")
        soft = sem("soft")
        neg_m_ready = sem("neg_m_ready")
        sink_m_ready = sem("sink_m_ready")
        probs_ready = sem("probs_ready")
        sink_e_ready = sem("sink_e_ready")
        probs_turned = sem("probs_turned")
        probsT_a = sem("probsT_a")
        probsT_b = sem("probsT_b")
        pv_done = sem("pv_done")
        att_ready = sem("att_ready")
        att_turned = sem("att_turned")
        attT_hi_ready = sem("attT_hi_ready")
        attT_lo_ready = sem("attT_lo_ready")
        rot = sem("rot")
        gate_ready = sem("gate_ready")
        rqk_turned = sem("rqk_turned")
        rqT_ready = sem("rqT_ready")
        rkT_ready = sem("rkT_ready")
        scores_done = sem("scores_done")
        scores_ready = sem("scores_ready")
        ret_done = sem("ret_done")
        stats_done = sem("stats_done")
        mv_ready = sem("mv_ready")
        var_eps_ready = sem("var_eps_ready")
        gn_ready = sem("gn_ready")
        y_raw_ready = sem("y_raw_ready")
        y_ready = sem("y_ready")
        y_turned = sem("y_turned")
        retT_hi_ready = sem("retT_hi_ready")
        retT_lo_ready = sem("retT_lo_ready")
        last_done = sem("last_done")
        x_final = sem("x_final")
        x_weighted = sem("x_weighted")
        out_ready = [sem(f"out_ready{t}") for t in range(T)]
        stored = sem("stored")

        block = ctx.enter_context(nc.Block())

        def x_bank(norm, p):
            return (2, 3, 4, 5, 6, 7, 2, 3)[p] if norm == FFN1 else (0, 1, 2, 3, 4, 5, 2, 3)[p]

        def f32(ap):
            return ap.bitcast(F32)

        def rot_view(half, head):
            qk = proj[:, :, R_Q:R_V].rearrange("p t (q h d) -> p t q h d", q=2, h=RH)
            return qk[:, :, :, head, half * (RD // 2):(half + 1) * (RD // 2)]

        @block.sync
        def _(sp):
            def load(g, s, src, width=W):
                if not (isinstance(g, int) and g == 0):
                    sp.wait_ge(lo_ready, 8 * g + 2 * s - 6)
                dst = raw[:, s, :].rearrange("p (k c) -> p k c", k=4)[:, :, 0:width]
                sp.dma_start(dst, src).then_inc(raw_loaded[s], 16)

            def rows(w, r0, c0, width=W):
                return w[bass.ds(r0, 4 * P), bass.ds(c0, width)].rearrange("(k p) c -> p k c", p=P)

            def load_ffn_in(f, g, i, loaded=0):
                for part in range(2):
                    for s in range(4):
                        if 4 * part + s >= loaded:
                            load(g + part, s, rows(ffn_w[f][part], 4 * P * s, i * W))

            def load_ffn_down(f, g, i):
                for s in range(4):
                    load(g, s, rows(ffn_w[f][2], i * W, s * W))

            def load_ffn(f):
                load_ffn_in(f, G_FFN[f], 0, 2 * (f == 0))
                if f == 0:
                    for t, t_d in ((sinks, sinks_d), (gn_w, gn_d), (cos, cos_d), (sin, sin_d), (decay, decay_d)):
                        sp.dma_start(t[:], t_d).then_inc(mix_consts, 16)
                else:
                    sp.wait_ge(retT_lo_ready, RH)
                    sp.dma_start(final_w, fw_d.partition_broadcast(P)).then_inc(fw_loaded, 16)
                with sp.Fori(1, NF) as i:
                    g = 3 * i + (G_FFN[f] - 1)
                    load_ffn_in(f, g, i)
                    load_ffn_down(f, g + 2, i - 1)
                load_ffn_down(f, G_FFN[f] + 3 * NF - 1, NF - 1)

            xv = x_d.rearrange("(t p) c -> p t c", p=P)
            sp.dma_start(ident[:], ident_d).then_inc(consts_loaded, 16)
            sp.dma_start(norms[:], norms_d).then_inc(consts_loaded, 16)
            for i, (kt0, kt1) in enumerate(X_PIECES):
                cols = slice(kt0 * P, kt1 * P)
                sp.dma_start(x[:, :, cols], xv[:, :, cols]).then_inc(x_loaded[i], 16)
                if i < 2:
                    sp.dma_start(raw[:, 0, i * HALF:(i + 1) * HALF].rearrange("p (k c) -> p k c", k=2),
                                 g1[2 * P * i:2 * P * (i + 1), 0:W].rearrange("(k p) c -> p k c", p=P)
                                 ).then_inc((first_half_loaded, raw_loaded[0])[i], 16)
                if i == 2:
                    load(0, 1, rows(g1, 4 * P, 0))
            load_ffn(0)
            with sp.Fori(0, NI) as b:
                for s in range(4):
                    load(b + G_IN, s, rows(w_in, 4 * P * s, b * WI, WI), WI)
            for part in range(2):
                for n in range(ND):
                    for u in range(2):
                        s = 2 * (n % 2) + u
                        load(G_OUT + 2 * part + n // 2, s, rows(w_out, D // 2 * part + 4 * P * u, n * W))
            load_ffn(1)
            ov = out_d.rearrange("(t p) c -> p t c", p=P)
            for t in range(T):
                for n in range(ND):
                    sp.wait_ge(out_ready[t], n + 1)
                    sp.dma_start(ov[:, t, n * W:(n + 1) * W], normed[:, t, n * W:(n + 1) * W]).then_inc(stored, 16)
            sp.wait_ge(stored, 16 * T * ND)

        @block.tensor
        def _(pe):
            def half(g, k, a_hi, a_lo, kt, bank, first, last, width=W):
                pe.wait_ge(lo_ready, 8 * g + (k + 1))
                for j in range(2):
                    for t in range(T):
                        out = ps[:, bank + t, 0:width]
                        xh, xl = (a[:, kt + j, t * P:(t + 1) * P] for a in (a_hi, a_lo))
                        wh, wl = (w[:, k % LEAD, j, 0:width] for w in (w_hi, w_lo))
                        pe.matmul(out, xh, wh, start=first and j == 0, stop=False)
                        pe.matmul(out, xh, wl, start=False, stop=False)
                        mm = pe.matmul(out, xl, wh, start=False, stop=last and j == 1)
                mm.then_inc(half_used, 1)

            def turn(bank, col, src):
                return pe.transpose(ps[0:src.shape[1], bank, col:col + P], src, ident[:])

            def turn_x(norm, p):
                n = p // 2
                if norm == FFN1:
                    pe.wait_ge(x_loaded[X_PIECE_OF_PAIR[p]], 16)
                elif p % 2 == 0:
                    pe.wait_ge(x_added, {MIX: X_FFN[0] + 4 * (NF - 1), FFN2: X_OUT + 4}[norm] + n + 1)
                bank = x_bank(norm, p)
                if norm == FFN1:
                    if p >= 6:
                        pe.wait_ge(xT_lo_ready, p - 6 + 1)
                elif n == 3:
                    pe.wait_ge(xT_lo_ready, PAIRS * norm + p - 4 + 1)
                elif (norm, p) == (MIX, 0):
                    pe.wait_ge(silu_done, T * NF)
                elif (norm, p) == (MIX, 2):
                    pe.wait_ge(h_ready, T * NF)
                elif (norm, p) == (FFN2, 0):
                    pe.wait_ge(rkT_ready, RH)
                    pe.wait_ge(rqT_ready, RH)
                elif (norm, p) == (FFN2, 2):
                    pe.wait_ge(retT_lo_ready, RH)
                    pe.wait_ge(y_raw_ready, T * RH)
                for j in range(2):
                    for t in range(T):
                        kt = 2 * p + j
                        mm = turn(bank, j * SEQ + t * P, x[:, t, kt * P:(kt + 1) * P])
                mm.then_inc(xT_turned, 1)

            def wide(norm, g, bank, h_of=None):
                for k in range(8):
                    if norm is not None and bank == B_GATE:
                        pe.wait_ge(xT_lo_ready, PAIRS * norm + k + 1)
                    half(g, k, xT_hi, xT_lo, 2 * k, bank, k == 0, k == 7)
                    if norm is not None and bank == B_GATE and (0 if norm == FFN1 else 2) <= k < 6:
                        turn_x(norm, k + 2)
                    if h_of is not None and k == 1:
                        turn_h(*h_of)

            def turn_h(f, i, bank=B_DOWN):
                c = NF * f + i
                pe.wait_ge(h_ready, 2 * c + 2)
                if bank == B_DOWN:
                    pe.wait_ge(x_added, 4 * i + (X_FFN[f] - 1))
                for b in range(2):
                    for j in range(2):
                        for t in range(T):
                            mm = turn(bank + b, j * SEQ + t * P, h[:, t, (2 * b + j) * P:(2 * b + j + 1) * P])
                    mm.then_inc(hT_turned, 1)

            def down(f, g, i, last=False):
                pe.wait_ge(hT_lo_ready, 2 * (NF * f + i) + 2)
                for n in range(ND):
                    if n > 0:
                        pe.wait_ge(x_added, 4 * i + (X_FFN[f] + n - 1))
                    for u in range(2):
                        half(g, 2 * n + u, hT_hi, hT_lo, 2 * u, B_DOWN + 2 * (n % 2), u == 0, u == 1)
                    if last and n == 1:
                        turn_h(f, NF - 1, B_GATE)

            def last_down(f, g):
                i = NF - 1
                pe.wait_ge(hT_lo_ready, 2 * (NF * f + i) + 2)
                for n in range(ND if f == 0 else ND - LATE):
                    pe.wait_ge(x_added, 4 * i + (X_FFN[f] + n - 1))
                    bank = B_DOWN + 2 * (n % 2)
                    for u in range(2):
                        half(g, 2 * n + u, last_hT_hi, last_hT_lo, 2 * u, bank, u == 0, u == 1)
                    if f == 0 and n in (1, 2):
                        turn_x(MIX, 2 * n - 2)
                        turn_x(MIX, 2 * n - 1)
                if f == 0:
                    for p in range(4, PAIRS):
                        turn_x(MIX, p)
                    return
                for t in range(T):
                    for n in range(ND - LATE, ND):
                        if t == 0:
                            pe.wait_ge(x_added, 4 * i + (X_FFN[f] + n - 1))
                        for kt in range(4):
                            if t == 0 and kt % 2 == 0:
                                pe.wait_ge(lo_ready, 8 * g + 2 * n + kt // 2 + 1)
                            out = ps[:, B_DOWN + 2 * (n % 2) + t, :]
                            wh, wl = (w[:, (2 * n + kt // 2) % LEAD, kt % 2, :] for w in (w_hi, w_lo))
                            xh, xl = (a[:, kt, t * P:(t + 1) * P] for a in (last_hT_hi, last_hT_lo))
                            pe.matmul(out, xh, wh, start=kt == 0, stop=False)
                            pe.matmul(out, xh, wl, start=False, stop=False)
                            mm = pe.matmul(out, xl, wh, start=False, stop=kt == 3)
                        mm.then_inc(last_done, 1)

            def ffn(f):
                norm = (FFN1, FFN2)[f]
                wide(norm, G_FFN[f], B_GATE)
                wide(norm, G_FFN[f] + 1, B_UP)

                def step(i, last=False):
                    g = 3 * i + (G_FFN[f] - 1)
                    pe.wait_ge(silu_done, 2 * i + T * NF * f)
                    wide(None, g, B_GATE, h_of=(f, i - 1))
                    pe.wait_ge(h_ready, 2 * i + T * NF * f)
                    wide(None, g + 1, B_UP)
                    down(f, g + 2, i - 1, last)

                with pe.Fori(1, NF - 1) as i:
                    step(i)
                step(NF - 1, last=True)
                last_down(f, G_FFN[f] + 3 * NF - 1)

            def logits(quad):
                pe.wait_ge(kT_ready, 3)
                pe.wait_ge(qT_ready, quad)
                pe.wait_ge(kT_in_ready, quad)
                for t in range(T):
                    for hh in range(QUAD):
                        for c in range(2):
                            n = CH if t == 0 and c == 0 else 2 * CH
                            mm = pe.matmul(ps[c * CH:(c + 1) * CH, B_DOWN + 2 + t, hh * P:hh * P + n],
                                           qT[:, t, hh * P + c * CH:hh * P + (c + 1) * CH],
                                           kT[:, t, c, 0:n], start=True, stop=True)
                mm.then_inc(logits_ready, 1)

            def weigh(quad):
                pe.wait_ge(probsT_a, quad)
                pe.wait_ge(probsT_b, quad)
                pe.wait_ge(v_in_ready, quad)
                for t in range(T):
                    for hh in range(QUAD):
                        for c in range(2):
                            col = (t * QUAD + hh) * HD
                            mm = pe.matmul(ps[c * CH:(c + 1) * CH, B_DOWN + 2, col:col + HD],
                                           probsT[:, t, hh * P + c * CH:hh * P + (c + 1) * CH],
                                           v[:, t, c, :], start=True, stop=True)
                mm.then_inc(pv_done, 1)

            def in_projection():
                def pair(i, quad=None):
                    for e in range(2):
                        pe.wait_ge(proj_ready, 2 * i + (e + 1))
                        for k in range(8):
                            if quad is None and e == 0:
                                pe.wait_ge(xT_lo_ready, PAIRS * MIX + k + 1)
                            if quad is not None and (e, k) == (0, 3):
                                pe.wait_ge(attT_lo_ready, quad)
                            half(2 * i + (G_IN + e), k, xT_hi, xT_lo, 2 * k, B_GATE + 2 * e, k == 0, k == 7, WI)
                            if quad is not None and (e, k) == (0, 1):
                                pe.wait_ge(kT_ready, 3)
                                pe.wait_ge(q_in_ready, quad)
                                for t in range(T):
                                    for hh in range(QUAD):
                                        mm = turn(B_DOWN + t, hh * P, q_in[:, t, hh * HD:(hh + 1) * HD])
                                mm.then_inc(q_turned, 1)
                            if quad is not None and (e, k) == (0, 3):
                                logits(quad)
                            if quad is not None and (e, k) == (1, 0):
                                pe.wait_ge(probs_ready, quad)
                                for t in range(T):
                                    for hh in range(QUAD):
                                        mm = turn(B_DOWN + t, hh * P, probs[:, t, hh, :])
                                mm.then_inc(probs_turned, 1)
                            if quad is not None and (e, k) == (1, 2):
                                weigh(quad)
                            if quad is not None and (e, k) == (1, 5):
                                pe.wait_ge(att_ready, quad)
                                for k2 in range(2):
                                    for t in range(T):
                                        mm = turn(B_DOWN + 3, k2 * SEQ + t * P, att[:, t, k2 * P:(k2 + 1) * P])
                                mm.then_inc(att_turned, 1)

                with pe.Fori(0, 2) as i:
                    pair(i)
                pe.wait_ge(proj_ready, 2 + 3)
                for g in range(KV):
                    for t in range(T):
                        mm = turn(B_DOWN, (g * T + t) * P, proj[:, t, A_K + g * HD:A_K + (g + 1) * HD])
                mm.then_inc(k_turned, 1)
                with pe.Fori(1, NQ + 1) as quad:
                    pair(quad + 1, quad)

            def retention_start(hd):
                pe.wait_ge(rot, 6 * (hd + 1))
                pe.wait_ge(proj_ready, 2 + NI)
                if hd:
                    pe.wait_ge(rqT_ready, hd)
                    pe.wait_ge(rkT_ready, hd)
                for qk in range(2):
                    for dt in range(2):
                        for t in range(T):
                            c0 = R_Q + qk * RH * RD + hd * RD + dt * P
                            mm = turn(B_GATE + qk, dt * SEQ + t * P, proj[:, t, c0:c0 + P])
                mm.then_inc(rqk_turned, 1)

            def retention_scores(hd):
                pe.wait_ge(rqT_ready, hd + 1)
                pe.wait_ge(rkT_ready, hd + 1)
                if hd:
                    pe.wait_ge(retT_lo_ready, hd)
                for m in range(T):
                    for dt in range(2):
                        mm = pe.matmul(ps[:, B_UP, 2 * P * m:2 * P * m + SEQ - m * P], rkT[:, dt, m * P:(m + 1) * P],
                                       rqT[:, dt, m * P:SEQ], start=dt == 0, stop=dt == 1)
                mm.then_inc(scores_done, 1)

            def retention_out(hd):
                pe.wait_ge(scores_ready, hd + 1)
                if hd:
                    pe.wait_ge(y_raw_ready, T * hd)
                for t in range(T):
                    for m in range(t + 1):
                        c0 = 2 * P * m + (t - m) * P
                        mm = pe.matmul(ps[:, B_UP + 1, t * RD:(t + 1) * RD], scores[:, c0:c0 + P],
                                       proj[:, m, R_V + hd * RD:R_V + (hd + 1) * RD], start=m == 0, stop=m == t)
                mm.then_inc(ret_done, 1)

            def retention_turn(hd):
                pe.wait_ge(y_ready, hd + 1)
                for k2 in range(2):
                    for t in range(T):
                        mm = turn(B_UP, k2 * SEQ + t * P, y[:, t, k2 * P:(k2 + 1) * P])
                mm.then_inc(y_turned, 1)

            def warm_up(products):
                for _ in range(products):
                    pe.matmul(ps[:, 0, :], junk[:, 0, 0:P], junk[:, 0, :], start=True, stop=True)

            pe.wait_ge(zeros_ready, 1)
            warm_up(8)
            pe.wait_ge(consts_loaded, 32)
            for p in range(2):
                turn_x(FFN1, p)
                warm_up(3)
            ffn(0)
            in_projection()
            for q in range(32):
                n, k = q // 4 % ND, q % 4
                if q < 16:
                    if n == 0:
                        pe.wait_ge(attT_lo_ready, 1 + k + 1)
                    if n >= 2 and k == 0:
                        pe.wait_ge(x_added, X_OUT + n - 1)
                    half(G_OUT, q, attT_hi, attT_lo, 2 * k, B_DOWN + 2 * (n % 2), k == 0, k == 3)
                else:
                    if n == 0:
                        pe.wait_ge(retT_lo_ready, k + 1)
                    if k == 0:
                        pe.wait_ge(x_added, X_OUT + 4 + n - 1)
                    half(G_OUT, q, xT_hi, xT_lo, 8 + 2 * k, B_DOWN + 2 * (n % 2), k == 0, k == 3)
                if q < 16:
                    if k == 0:
                        retention_start(n)
                    if k == 2:
                        retention_scores(n)
                    if k == 3:
                        retention_out(n)
                if q % 4 == 1 and 5 <= q <= 17:
                    retention_turn(q // 4 - 1)
                if q in (22, 26):
                    for p in range(2):
                        turn_x(FFN2, (q - 22) // 2 + p)
            ffn(1)

        @block.scalar
        def _(act):
            def split(g, k, first=False):
                g, k = g + k // 8, k % 8
                s = k // 2
                if not first:
                    act.wait_ge(half_used, 8 * g + (k + 1 - LEAD))
                if first and k == 0:
                    act.wait_ge(first_half_loaded, 16)
                elif k % 2 == 0 or (first and k == 1):
                    act.wait_ge(raw_loaded[s], 16 * g + 16)
                dst = w_hi[:, k % LEAD, :, :].rearrange("p k c -> p (k c)")
                act.activation(dst, raw[:, s, (k % 2) * HALF:(k % 2 + 1) * HALF], ACT.Copy).then_inc(hi_ready, 1)

            def position(g, k):
                if not (isinstance(g, int) and 8 * g + k + LEAD >= HALVES):
                    split(g, k + LEAD)

            def xT(norm, p):
                act.wait_ge(xT_turned, PAIRS * norm + p + 1)
                for j in range(2):
                    kt = 2 * p + j
                    a = act.activation(xT_hi[:, kt, :], ps[:, x_bank(norm, p), j * SEQ:(j + 1) * SEQ],
                                       ACT.Copy, scale=norms[:, norm, kt:kt + 1])
                a.then_inc(xT_hi_ready, 1)

            def square(norm, n, t, count):
                if count > 1:
                    act.wait_ge(sq_ready, count - 1)
                act.activation(junk[:, count % 2, :], x[:, t, n * W:(n + 1) * W], ACT.Square,
                               accum_out=sq[:, norm, t, n:n + 1]).then_inc(sq_ready, 1)

            def squares(norm, n):
                if norm == FFN1:
                    for p in range(2):
                        act.wait_ge(x_loaded[X_PIECE_OF_PAIR[2 * n + p]], 16)
                else:
                    act.wait_ge(x_added, {MIX: X_FFN[0] + 4 * (NF - 1), FFN2: X_OUT + 4,
                                          FINAL: X_FFN[1] + 4 * (NF - 1)}[norm] + n + 1)
                for t in range(T):
                    square(norm, n, t, T * (ND * norm + n) + t)

            def silu(f, g, i):
                act.wait_ge(half_used, 8 * g + 8)
                for t in range(T):
                    if not (isinstance(i, int) and f == 0):
                        act.wait_ge(h_ready, 2 * i + (T * NF * f + t - 1))
                    act.activation(sg[:, t, :], ps[:, B_GATE + t, :], ACT.Silu,
                                   scale=rstd[:, (FFN1, FFN2)[f], t:t + 1]).then_inc(silu_done, 1)

            def hT(f, i, dst=hT_hi, bank=B_DOWN):
                for b in range(2):
                    act.wait_ge(hT_turned, 2 * i + (T * NF * f + b + 1))
                    act.activation(dst[:, 2 * b:2 * b + 2, :].rearrange("p k s -> p (k s)"), ps[:, bank + b, :],
                                   ACT.Copy).then_inc(hT_hi_ready, 1)

            def ffn(f):
                g0 = G_FFN[f]
                norm = (FFN1, FFN2)[f]
                for k in range(16):
                    if 1 <= k < 5:
                        xT(norm, k + 3)
                    position(g0, k)
                    if 4 <= k < 8 and (f == 0 or k >= 6):
                        squares(norm, k - 4)
                    if k == 9:
                        act.wait_ge(rstd_ready, (FFN1, FFN2)[f] + 1)
                        silu(f, g0, 0)

                def step(i, last=False):
                    g = 3 * i + (g0 - 1)
                    for k in range(24):
                        position(g, k)
                        if k == 1:
                            hT(f, i - 1)
                        if k == 7:
                            silu(f, g, i)
                        if last and k == 19:
                            hT(f, i, last_hT_hi, B_GATE)

                with act.Fori(1, NF - 1) as i:
                    step(i)
                step(NF - 1, last=True)
                g = g0 + 3 * NF - 1
                for k in range(8):
                    position(g, k)
                    if f == 0:
                        if k in (3, 5):
                            xT(MIX, k - 3)
                            xT(MIX, k - 2)
                            squares(MIX, (k - 3) // 2)
                        if k == 7:
                            for p in range(4, PAIRS):
                                xT(MIX, p)
                            for n in (2, 3):
                                squares(MIX, n)
                    elif k in (2, 3):
                        squares(FINAL, k - 2)

            def proj_out(b, bank):
                act.wait_ge(half_used, 8 * b + (8 * G_IN + 8))
                for t in range(T):
                    a = act.activation(proj[:, t, bass.ds(b * WI, WI)], ps[:, bank + t, 0:WI], ACT.Copy,
                                       scale=rstd[:, MIX, t:t + 1])
                a.then_inc(proj_ready, 1)

            def in_pair(i, j=None):
                for k in range(16):
                    position(2 * i + G_IN, k)
                    if k == 7:
                        proj_out(2 * i, B_GATE)
                    if k == 15:
                        proj_out(2 * i + 1, B_UP)
                    if j is None:
                        continue
                    if k == 1:
                        act.wait_ge(q_turned, j + 1)
                        act.activation(qT.rearrange("p t c -> p (t c)"),
                                       ps[0:HD, B_DOWN:B_DOWN + 2, :].rearrange("p t c -> p (t c)"),
                                       ACT.Copy).then_inc(qT_ready, 1)
                    if k == 4:
                        act.wait_ge(neg_m_ready, j + 1)
                        for t in range(T):
                            for hh in range(QUAD):
                                c = t * QUAD + hh
                                a = act.activation(probs[:, t, hh, :], ps[:, B_DOWN + 2 + t, hh * P:(hh + 1) * P],
                                                   ACT.Exp, bias=neg_m[:, c:c + 1], scale=HD ** -0.5,
                                                   accum_out=den[:, c:c + 1])
                        a.then_inc(probs_ready, 1)
                        act.wait_ge(sink_m_ready, j + 1)
                        act.activation(sink_e[:], sink_m[:], ACT.Exp).then_inc(sink_e_ready, 1)
                    if k == 8:
                        act.wait_ge(probs_turned, j + 1)
                        act.activation(probsT[:, 0, :], ps[:, B_DOWN, :], ACT.Copy).then_inc(probsT_a, 1)
                    if k == 13:
                        act.wait_ge(att_turned, j + 1)
                        act.activation(attT_hi[:, bass.ds(2 * j, 2), :], ps[:, B_DOWN + 3, :].rearrange(
                            "p (k s) -> p k s", k=2), ACT.Copy).then_inc(attT_hi_ready, 1)

            act.wait_ge(consts_loaded, 32)
            act.sem_inc(proj_ready, 2)
            for k in range(LEAD):
                xT(FFN1, k)
                split(0, k, first=True)
            ffn(0)
            act.wait_ge(rstd_ready, MIX + 1)
            with act.Fori(0, 2) as i:
                in_pair(i)
            with act.Fori(0, NQ) as j:
                in_pair(j + 2, j)
            for q in range(32):
                if q % 4 == 1 and 5 <= q <= 17:
                    hd = q // 4 - 1
                    act.wait_ge(y_turned, hd + 1)
                    for k2 in range(2):
                        a = act.activation(xT_hi[:, 8 + 2 * hd + k2, :], ps[:, B_UP, k2 * SEQ:(k2 + 1) * SEQ],
                                           ACT.Copy, scale=gn_w[:, 2 * hd + k2:2 * hd + k2 + 1])
                    a.then_inc(retT_hi_ready, 1)
                position(G_OUT, q)
                if q % 4 == 0 and q < 16:
                    hd = q // 4
                    act.wait_ge(rqk_turned, hd + 1)
                    act.activation(rqT.rearrange("p k s -> p (k s)"), ps[:, B_GATE, :],
                                   ACT.Copy).then_inc(rqT_ready, 1)
                    gate = proj[:, :, R_G + hd * RD:R_G + (hd + 1) * RD]
                    if hd == 0:
                        act.wait_ge(proj_ready, 2 + NI)
                    act.activation(gate, gate, ACT.Silu).then_inc(gate_ready, 1)
                if q % 4 == 0 and 4 <= q <= 16:
                    hd = q // 4 - 1
                    act.wait_ge(gn_ready, hd + 1)
                    act.wait_ge(y_raw_ready, T * (hd + 1))
                    if hd:
                        act.wait_ge(y_turned, hd)
                    for t in range(T):
                        a = act.activation(y[:, t, :], y_raw[:, t, :], ACT.Copy, scale=gn_rstd[:, hd, t:t + 1])
                    a.then_inc(y_ready, 1)
                if q in (22, 26):
                    for p in range(2):
                        xT(FFN2, (q - 22) // 2 + p)
                    squares(FFN2, (q - 22) // 4)
            ffn(1)

            def scale_first(n):
                yb = normed[:, 0, n * W:(n + 1) * W]
                act.activation(yb, yb, ACT.Copy, scale=rstd[:, FINAL, 0:1]).then_inc(out_ready[0], 1)

            def late_square(t, i):
                act.wait_ge(x_final, LATE * t + i + 1)
                square(FINAL, ND - LATE + i, t, T * (ND * FINAL + ND - LATE) + LATE * t + i)

            for i in range(LATE):
                late_square(0, i)
            act.wait_ge(rstd_ready, FINAL + 1)
            act.wait_ge(x_weighted, T * (ND - LATE) + LATE)
            for n in range(ND):
                scale_first(n)
                if n % 2:
                    late_square(1, n // 2)

        @block.vector
        def _(dve):
            def split(g, k):
                g, k = g + k // 8, k % 8
                dve.wait_ge(hi_ready, 8 * g + (k + 1))
                flat = "p k c -> p (k c)"
                dve.tensor_tensor(w_lo[:, k % LEAD, :, :].rearrange(flat),
                                  raw[:, k // 2, (k % 2) * HALF:(k % 2 + 1) * HALF],
                                  f32(w_hi[:, k % LEAD, :, :].rearrange(flat)), ALU.subtract).then_inc(lo_ready, 1)

            def position(g, k):
                if not (isinstance(g, int) and 8 * g + k + LEAD >= HALVES):
                    split(g, k + LEAD)

            def xT(norm, p):
                dve.wait_ge(xT_hi_ready, PAIRS * norm + p + 1)
                for j in range(2):
                    kt = 2 * p + j
                    a = dve.scalar_tensor_tensor(out=xT_lo[:, kt, :],
                                                 in0=ps[:, x_bank(norm, p), j * SEQ:(j + 1) * SEQ],
                                                 scalar=norms[:, norm, kt:kt + 1], in1=f32(xT_hi[:, kt, :]),
                                                 op0=ALU.mult, op1=ALU.subtract)
                a.then_inc(xT_lo_ready, 1)

            def mean_square(norm, t0=0, t1=T):
                done = T * ND * norm + (T * ND if norm != FINAL else T * (ND - LATE) + LATE * t1)
                dve.wait_ge(sq_ready, done)
                dve.tensor_reduce(ms[:, norm, t0:t1], sq[:, norm, t0:t1, :], AX.X, ALU.add).then_inc(ms_added, 1)
                dve.wait_ge(ms_added, norm + t0 + 1)
                dve.tensor_scalar(ms_eps[:, norm, t0:t1], ms[:, norm, t0:t1], 1.0 / D, EPS, ALU.mult,
                                  ALU.add).then_inc(ms_ready, 1)

            def gated(f, g, i):
                dve.wait_ge(half_used, 8 * g + 16)
                for t in range(T):
                    dve.wait_ge(silu_done, 2 * i + (T * NF * f + t + 1))
                    if not (isinstance(i, int) and f == 0) and t == 0:
                        dve.wait_ge(hT_turned, 2 * i + T * NF * f)
                    dve.scalar_tensor_tensor(out=h[:, t, :], in0=ps[:, B_UP + t, :],
                                             scalar=rstd[:, (FFN1, FFN2)[f], t:t + 1], in1=sg[:, t, :],
                                             op0=ALU.mult, op1=ALU.mult).then_inc(h_ready, 1)

            def hT(f, i, hi=hT_hi, lo=hT_lo, bank=B_DOWN):
                for b in range(2):
                    dve.wait_ge(hT_hi_ready, 2 * i + (T * NF * f + b + 1))
                    dve.tensor_tensor(lo[:, 2 * b:2 * b + 2, :].rearrange("p k s -> p (k s)"), ps[:, bank + b, :],
                                      f32(hi[:, 2 * b:2 * b + 2, :].rearrange("p k s -> p (k s)")),
                                      ALU.subtract).then_inc(hT_lo_ready, 1)

            def add(g, k, n, scale):
                dve.wait_ge(half_used, 8 * g + (k + 1))
                for t in range(T):
                    xb = x[:, t, n * W:(n + 1) * W]
                    a = dve.scalar_tensor_tensor(out=xb, in0=ps[:, B_DOWN + 2 * (n % 2) + t, :], scalar=scale,
                                                 in1=xb, op0=ALU.mult, op1=ALU.add)
                a.then_inc(x_added, 1)

            def ffn(f):
                g0 = G_FFN[f]
                for k in range(16):
                    if 1 <= k < 5:
                        xT((FFN1, FFN2)[f], k + 3)
                    position(g0, k)
                    if k == 8:
                        mean_square((FFN1, FFN2)[f])
                    if k == 15:
                        dve.wait_ge(rstd_ready, (FFN1, FFN2)[f] + 1)
                        gated(f, g0, 0)

                def step(i, last=False):
                    g = 3 * i + (g0 - 1)
                    for k in range(24):
                        position(g, k)
                        if k == 1:
                            hT(f, i - 1)
                        if k == 15:
                            gated(f, g, i)
                        if k >= 16 and k % 2:
                            add(g, k, (k - 16) // 2, 0.5)
                        if last and k == 19:
                            hT(f, i, last_hT_hi, last_hT_lo, B_GATE)

                with dve.Fori(1, NF - 1) as i:
                    step(i)
                step(NF - 1, last=True)
                g = g0 + 3 * NF - 1
                if f == 1:
                    dve.wait_ge(fw_loaded, 16)
                for k in range(8 if f == 0 else 2 * (ND - LATE)):
                    late = k == (7 if f == 0 else 3)
                    if not late:
                        position(g, k)
                    if k % 2:
                        add(g, k, k // 2, 0.5)
                    if late and f == 1:
                        position(g, k)
                    if f == 1 and k % 2:
                        for t in range(T):
                            weigh_final(t, k // 2)
                    if f == 0 and k in (3, 5):
                        xT(MIX, k - 3)
                        xT(MIX, k - 2)
                    if f == 0 and k == 7:
                        xT(MIX, 4)
                        xT(MIX, 5)
                        position(g, k)
                        xT(MIX, 6)
                        xT(MIX, 7)
                        mean_square(MIX)

            def weigh_final(t, n):
                cols = slice(n * W, (n + 1) * W)
                if t == 0 and n < ND - LATE:
                    dve.wait_ge(x_added, X_FFN[1] + 4 * (NF - 1) + n + 1)
                dve.tensor_tensor(normed[:, t, cols], x[:, t, cols], final_w[:, cols],
                                  ALU.mult).then_inc(x_weighted, 1)

            def in_pair(i, j=None):
                for k in range(16):
                    position(2 * i + G_IN, k)
                    if j is None:
                        continue
                    if k == 3:
                        dve.wait_ge(logits_ready, j + 1)
                        first = ps[0:CH, B_DOWN + 2, :].rearrange("p (h c) -> p h c", h=QUAD)
                        dve.memset(first[:, :, CH:2 * CH], -3.0e38).then_inc(soft, 1)
                        dve.wait_ge(soft, 4 * j + 1)
                        dve.tensor_reduce(lmax[:], ps[:, B_DOWN + 2:B_DOWN + 4, :].rearrange(
                            "p t (h c) -> p (t h) c", h=QUAD), AX.X, ALU.max).then_inc(soft, 1)
                        dve.wait_ge(soft, 4 * j + 2)
                        dve.scalar_tensor_tensor(out=neg_m[:], in0=lmax[:], scalar=-HD ** -0.5,
                                                 in1=neg_sinks[:, bass.ds(8 * j, 8)], op0=ALU.mult,
                                                 op1=ALU.min).then_inc(neg_m_ready, 1)
                        dve.wait_ge(neg_m_ready, j + 1)
                        dve.tensor_tensor(sink_m[:], sinks[:, bass.ds(8 * j, 8)], neg_m[:],
                                          ALU.add).then_inc(sink_m_ready, 1)
                    if k == 8:
                        dve.wait_ge(sink_e_ready, j + 1)
                        dve.tensor_tensor(den2[:], den[:], sink_e[:], ALU.add).then_inc(soft, 1)
                        dve.wait_ge(soft, 4 * j + 3)
                        dve.reciprocal(rden[:], den2[:]).then_inc(soft, 1)
                        dve.wait_ge(probs_turned, j + 1)
                        dve.tensor_copy(probsT[:, 1, :], ps[:, B_DOWN + 1, :]).then_inc(probsT_b, 1)
                    if k == 10:
                        dve.wait_ge(pv_done, j + 1)
                        dve.wait_ge(soft, 4 * j + 4)
                        dve.tensor_tensor(att[:].rearrange("p t (h d) -> p (t h) d", h=QUAD),
                                          ps[:, B_DOWN + 2, :].rearrange("p (h d) -> p h d", d=HD),
                                          rden[:].unsqueeze(2).to_broadcast([P, T * QUAD, HD]),
                                          ALU.mult).then_inc(att_ready, 1)
                    if k == 13:
                        dve.wait_ge(attT_hi_ready, j + 1)
                        dve.tensor_tensor(attT_lo[:, bass.ds(2 * j, 2), :],
                                          ps[:, B_DOWN + 3, :].rearrange("p (k s) -> p k s", k=2),
                                          f32(attT_hi[:, bass.ds(2 * j, 2), :]),
                                          ALU.subtract).then_inc(attT_lo_ready, 1)

            dve.memset(junk[:], 0.0).then_inc(zeros_ready, 1)
            dve.sem_inc(x_added, X_FFN[0])
            dve.sem_inc(attT_lo_ready, 1)
            dve.wait_ge(consts_loaded, 32)
            for k in range(LEAD):
                xT(FFN1, k)
                split(0, k)
            ffn(0)
            dve.wait_ge(mix_consts, 16 * 5)
            dve.tensor_scalar(neg_sinks[:], sinks[:], -1.0, None, ALU.mult).then_inc(neg_sinks_ready, 1)
            with dve.Fori(0, 2) as i:
                in_pair(i)
            dve.wait_ge(k_turned, 1)
            dve.wait_ge(kT_zeroed, 1)
            turned = ps[0:HD, B_DOWN, :].rearrange("p (g t c) -> p g t c", g=KV, t=T)
            dve.tensor_copy(kT_all[:, :, :, 1, :], turned).then_inc(kT_ready, 1)
            dve.tensor_copy(kT_all[:, :, :, 0, 0:CH], turned[:, :, :, 0:CH]).then_inc(kT_ready, 1)
            dve.tensor_copy(kT_all[:, :, 1, 0, CH:2 * CH], turned[:, :, 0, CH:2 * CH]).then_inc(kT_ready, 1)
            dve.wait_ge(neg_sinks_ready, 1)
            with dve.Fori(0, NQ) as j:
                in_pair(j + 2, j)
            for q in range(32):
                if q % 4 == 1 and 5 <= q <= 17:
                    hd = q // 4 - 1
                    dve.wait_ge(retT_hi_ready, hd + 1)
                    for k2 in range(2):
                        a = dve.scalar_tensor_tensor(
                            out=xT_lo[:, 8 + 2 * hd + k2, :], in0=ps[:, B_UP, k2 * SEQ:(k2 + 1) * SEQ],
                            scalar=gn_w[:, 2 * hd + k2:2 * hd + k2 + 1], in1=f32(xT_hi[:, 8 + 2 * hd + k2, :]),
                            op0=ALU.mult, op1=ALU.subtract)
                    a.then_inc(retT_lo_ready, 1)
                position(G_OUT, q)
                if q % 4 == 3:
                    add(G_OUT, q, q // 4 % ND, 1.0)
                if q % 4 == 0 and q < 16:
                    hd = q // 4
                    dve.wait_ge(rqk_turned, hd + 1)
                    dve.tensor_copy(rkT.rearrange("p k s -> p (k s)"), ps[:, B_GATE + 1, :]).then_inc(rkT_ready, 1)
                if q % 4 == 2 and q < 16:
                    hd = q // 4
                    dve.wait_ge(scores_done, hd + 1)
                    dve.tensor_tensor(scores, ps[:, B_UP, 0:3 * P], decay[:, hd, :], ALU.mult).then_inc(scores_ready, 1)
                if q % 4 == 3 and q < 16:
                    hd = q // 4
                    dve.wait_ge(ret_done, hd + 1)
                    for t in range(T):
                        dve.bn_stats(stats[:, hd, t, :], ps[:, B_UP + 1, t * RD:(t + 1) * RD]).then_inc(stats_done, 1)
                    for t in range(T):
                        dve.wait_ge(stats_done, T * hd + t + 1)
                        dve.bn_aggr(mv[:, hd, t, :], stats[:, hd, t, :]).then_inc(mv_ready, 1)
                    dve.wait_ge(gate_ready, hd + 1)
                    dve.wait_ge(mv_ready, T * (hd + 1))
                    if hd:
                        dve.wait_ge(y_ready, hd)
                    for t in range(T):
                        dve.scalar_tensor_tensor(out=y_raw[:, t, :], in0=ps[:, B_UP + 1, t * RD:(t + 1) * RD],
                                                 scalar=mv[:, hd, t, 0:1],
                                                 in1=proj[:, t, R_G + hd * RD:R_G + (hd + 1) * RD],
                                                 op0=ALU.subtract, op1=ALU.mult).then_inc(y_raw_ready, 1)
                if q in (22, 26):
                    for p in range(2):
                        xT(FFN2, (q - 22) // 2 + p)
            ffn(1)
            for t in range(T):
                for i in range(LATE):
                    n = ND - LATE + i
                    dve.wait_ge(last_done, LATE * t + i + 1)
                    xb = x[:, t, n * W:(n + 1) * W]
                    dve.scalar_tensor_tensor(out=xb, in0=ps[:, B_DOWN + 2 * (n % 2) + t, :], scalar=0.5, in1=xb,
                                             op0=ALU.mult, op1=ALU.add).then_inc(x_final, 1)
                    dve.wait_ge(x_final, LATE * t + i + 1)
                    weigh_final(t, n)
                mean_square(FINAL, t, t + 1)
            dve.wait_ge(rstd_ready, FINAL + T)
            dve.wait_ge(x_weighted, T * ND)
            for n in range(ND):
                yb = normed[:, 1, n * W:(n + 1) * W]
                dve.tensor_scalar(yb, yb, rstd[:, FINAL, 1:2], None, ALU.mult).then_inc(out_ready[1], 1)

        @block.gpsimd
        def _(pool):
            def rsqrt_of_norm(norm, t0=0, t1=T):
                pool.wait_ge(ms_ready, norm + t0 + 1)
                pool.tensor_tensor(rstd[:, norm, t0:t1], ms_eps[:, norm, t0:t1], minus_half[:, t0:t1],
                                   ALU.pow).then_inc(rstd_ready, 1)

            def stage(j):
                again = not isinstance(j, int)
                if again:
                    pool.wait_ge(q_turned, j)
                    pool.wait_ge(v_in_ready, j)
                pool.tensor_copy(q_in[:], proj[:, :, bass.ds(j * QUAD * HD, QUAD * HD)]).then_inc(q_in_ready, 1)
                if again:
                    pool.wait_ge(logits_ready, j)
                else:
                    pool.wait_ge(kT_ready, 3)
                pool.wait_ge(q_in_ready, j + 1)
                pool.tensor_copy(kT[:], kT_all[:, bass.ds(j // 2, 1), :, :, :].rearrange(
                    "p g t v c -> p (g t) v c")).then_inc(kT_in_ready, 1)
                if again:
                    pool.wait_ge(pv_done, j)
                pool.wait_ge(kT_in_ready, j + 1)
                pool.tensor_copy(v[:], v_all[:, bass.ds(j // 2, 1), :, :, :].rearrange(
                    "p g t v c -> p (g t) v c")).then_inc(v_in_ready, 1)

            def rotate(hd):
                t1, t2 = rot_view(0, hd), rot_view(1, hd)
                c, s = (a[:].unsqueeze(2).to_broadcast([P, T, 2, RD // 2]) for a in (cos, sin))
                step = 6 * hd
                if hd:
                    pool.wait_ge(rot, step)
                pool.tensor_tensor(rot_a, t1, s, ALU.mult).then_inc(rot, 1)
                pool.tensor_tensor(rot_b, t2, s, ALU.mult).then_inc(rot, 1)
                pool.wait_ge(rot, step + 2)
                pool.tensor_tensor(t1, t1, c, ALU.mult).then_inc(rot, 1)
                pool.tensor_tensor(t2, t2, c, ALU.mult).then_inc(rot, 1)
                pool.wait_ge(rot, step + 4)
                pool.tensor_tensor(t1, t1, rot_b, ALU.subtract).then_inc(rot, 1)
                pool.tensor_tensor(t2, t2, rot_a, ALU.add).then_inc(rot, 1)

            def rsqrt_of_head(hd):
                pool.wait_ge(mv_ready, T * (hd + 1))
                pool.tensor_scalar(var_eps[:, hd, :], mv[:, hd, :, 1], EPS, None, ALU.add).then_inc(var_eps_ready, 1)
                pool.wait_ge(var_eps_ready, hd + 1)
                pool.tensor_tensor(gn_rstd[:, hd, :], var_eps[:, hd, :], minus_half[:], ALU.pow).then_inc(gn_ready, 1)

            pool.memset(minus_half[:], -0.5).then_inc(half_const, 1)
            pool.wait_ge(half_const, 1)
            rsqrt_of_norm(FFN1)
            rsqrt_of_norm(MIX)
            pool.wait_ge(rstd_ready, MIX + 1)
            pool.memset(kT_all[:, :, 0, 0, CH:2 * CH], 0.0).then_inc(kT_zeroed, 1)
            pool.wait_ge(kT_zeroed, 1)
            pool.memset(v_all[CH:P, :, 0, 0, :], 0.0).then_inc(v_ready, 1)
            pool.wait_ge(proj_ready, 2 + 3)
            pool.wait_ge(v_ready, 1)
            vals = proj[:, :, A_V:R_Q].rearrange("p t (g d) -> p g t d", g=KV)
            pool.tensor_copy(v_all[:, :, :, 1, :], vals).then_inc(v_ready, 1)
            pool.wait_ge(v_ready, 2)
            pool.tensor_copy(v_all[0:CH, :, :, 0, :], vals[0:CH]).then_inc(v_ready, 1)
            pool.wait_ge(v_ready, 3)
            pool.tensor_copy(v_all[CH:P, :, 1, 0, :], vals[CH:P, :, 0, :]).then_inc(v_ready, 1)
            pool.wait_ge(v_ready, 4)
            stage(0)
            with pool.Fori(1, NQ) as j:
                stage(j)
            pool.wait_ge(v_in_ready, NQ)
            pool.wait_ge(proj_ready, 2 + 8)
            pool.wait_ge(mix_consts, 16 * 5)
            pool.wait_ge(logits_ready, NQ)
            for hd in range(RH):
                rotate(hd)
            for hd in range(RH):
                rsqrt_of_head(hd)
            rsqrt_of_norm(FFN2)
            for t in range(T):
                rsqrt_of_norm(FINAL, t, t + 1)


def constants():
    inv = np.float32(10000.0) ** (-np.arange(0, RD, 2, dtype=np.float32) / np.float32(RD))
    ang = np.arange(SEQ, dtype=np.float32)[:, None] * inv.astype(np.float32)[None, :]
    by_token = [f(ang).astype(np.float32).reshape(T, P, RD // 2).transpose(1, 0, 2) for f in (np.cos, np.sin)]
    log_gamma = np.log(1.0 - 2.0 ** (-5.0 - np.arange(RH, dtype=np.float64)))
    n = np.arange(SEQ)
    dist = n[None, :] - n[:, None]
    full = np.where(dist >= 0, np.exp(log_gamma[:, None, None] * np.maximum(dist, 0)), 0.0) * RD ** -0.5
    tiles = np.concatenate([full[:, 0:P, :], full[:, P:SEQ, P:SEQ]], axis=2)
    return {"ident": np.eye(P, dtype=np.float32), "cos": by_token[0], "sin": by_token[1],
            "decay": tiles.transpose(1, 0, 2).astype(np.float32)}


def kernel(**inputs):
    import concourse.bacc as bacc
    from concourse.bass_utils import run_bass_kernel_spmd

    a = {k: np.asarray(v) for k, v in inputs.items()}

    def by_feature(w, n):
        return w.reshape(n, P).T

    arrays = {
        "x": a["x"].reshape(SEQ, D),
        "norms": np.stack([by_feature(a[k], KT) for k in ("norm_ffn1_w", "norm_mix_w", "norm_ffn2_w")], axis=1),
        "g1": a["ffn1_w_gate"][0], "u1": a["ffn1_w_up"][0], "d1": a["ffn1_w_down"][0],
        "w_in": a["w_in"][0],
        "sinks": np.broadcast_to(a["attn_sinks"].reshape(1, NQ, 1, QUAD), (P, NQ, T, QUAD)).reshape(P, -1),
        "gn": by_feature(a["ret_gn_w"], 8),
        "w_out": a["w_out"][0],
        "g2": a["ffn2_w_gate"][0], "u2": a["ffn2_w_up"][0], "d2": a["ffn2_w_down"][0],
        "fw": a["norm_final_w"],
        **constants(),
    }
    nc = bacc.Bacc("TRN2", target_bir_lowering=False, num_devices=1)
    feed, args = {}, []
    for name, arr in arrays.items():
        arr = np.ascontiguousarray(arr)
        feed[f"in_{name}"] = arr
        args.append(nc.dram_tensor(f"in_{name}", arr.shape, mybir.dt.from_np(arr.dtype), kind="ExternalInput").ap())
    out = nc.dram_tensor("out", (SEQ, D), F32, kind="ExternalOutput").ap()
    build(nc, *args, out)
    r = run_bass_kernel_spmd(nc, [feed], core_ids=[0])
    return r.results[0]["out"].reshape(1, SEQ, D)
```
